# Optimizing a Trainium2 kernel written in Bass

```python
import math
import jax, jax.numpy as jnp
from jax import lax
import numpy as np

D_MODEL = 2048
BATCH = 1
SEQ = 512
DEPTH = 1
DEC_BATCH = 1
DEC_SEQ = 32
PAST_LEN = 256

CHUNK = 64
EPS = 1e-6
D_CONV = D_MODEL // 2
CONV_WIDTH = 31
CONV_STATE = CONV_WIDTH - 1
N_HEADS = 8
D_HEAD = 64
D_VHEAD = 2 * D_HEAD
D_ATTN = N_HEADS * D_VHEAD
ROPE_THETA = 10000.0
Q_BLOCK = 128
NEG_INF = -1e30
PEER_HEADS = 8
PEER_NKEYS = 128
PEER_EXPERTS = PEER_NKEYS * PEER_NKEYS
PEER_DKEY = 128
PEER_TOPK = 16
PEER_BLOCK = 128
OFF_GLU_A = 0
OFF_GLU_B = OFF_GLU_A + D_CONV
OFF_Q = OFF_GLU_B + D_CONV
OFF_K = OFF_Q + N_HEADS * 2 * D_HEAD
OFF_V = OFF_K + N_HEADS * 2 * D_HEAD
OFF_GATE_C = OFF_V + D_ATTN
OFF_GATE_A = OFF_GATE_C + D_MODEL
D_IN_PROJ = OFF_GATE_A + D_MODEL

kernel_name = "hybrid_conformer_diffattn_peer_stream_step"

def lambda_init(layer):
    return 0.8 - 0.6 * math.exp(-0.3 * layer)

def rms_norm(x, g):
    xf = x.astype(jnp.float32)
    y = xf * lax.rsqrt(jnp.mean(xf * xf, axis=-1, keepdims=True) + EPS)
    return (y * g.astype(jnp.float32)).astype(x.dtype)

def layer_norm(x, g, b):
    xf = x.astype(jnp.float32)
    mu = jnp.mean(xf, axis=-1, keepdims=True)
    var = jnp.mean(jnp.square(xf - mu), axis=-1, keepdims=True)
    y = (xf - mu) * lax.rsqrt(var + EPS)
    return (y * g.astype(jnp.float32) + b.astype(jnp.float32)).astype(x.dtype)

def rope(x, pos):
    half = D_HEAD // 2
    inv = ROPE_THETA ** (-jnp.arange(half, dtype=jnp.float32) / half)
    ang = pos.astype(jnp.float32)[:, None] * inv[None, :]
    cos = jnp.cos(ang)[:, None, None, :]
    sin = jnp.sin(ang)[:, None, None, :]
    xf = x.astype(jnp.float32)
    x1, x2 = xf[..., :half], xf[..., half:]
    return jnp.concatenate([x1 * cos - x2 * sin, x2 * cos + x1 * sin], axis=-1).astype(x.dtype)

def diff_core(q, k, v, mask, lam):
    s = jnp.einsum('bqhcd,bkhcd->bhcqk', q, k).astype(jnp.float32) * (D_HEAD ** -0.5)
    if mask is not None:
        s = jnp.where(mask[None, None, None], s, NEG_INF)
    p = jax.nn.softmax(s, axis=-1)
    a = p[:, :, 0] - lam * p[:, :, 1]
    return jnp.einsum('bhqk,bkhe->bqhe', a.astype(v.dtype), v)

def attn_branch(z, pos, k_past, v_past, p, lam_init):
    B_, T_, _ = z.shape
    q = z[..., OFF_Q:OFF_K].reshape(B_, T_, N_HEADS, 2, D_HEAD)
    k = z[..., OFF_K:OFF_V].reshape(B_, T_, N_HEADS, 2, D_HEAD)
    v = z[..., OFF_V:OFF_GATE_C].reshape(B_, T_, N_HEADS, D_VHEAD)
    q = rope(rms_norm(q, p['q_norm_g']), pos)
    k = rope(rms_norm(k, p['k_norm_g']), pos)
    f32 = jnp.float32
    lam = (jnp.exp(jnp.sum(p['lambda_q1'].astype(f32) * p['lambda_k1'].astype(f32)))
           - jnp.exp(jnp.sum(p['lambda_q2'].astype(f32) * p['lambda_k2'].astype(f32)))
           + lam_init)
    if k_past is None:
        nb = T_ // Q_BLOCK
        qb = jnp.moveaxis(q.reshape(B_, nb, Q_BLOCK, N_HEADS, 2, D_HEAD), 1, 0)
        k_chunk = jnp.arange(T_) // CHUNK

        def blk(args):
            qi, i = args
            q_chunk = (i * Q_BLOCK + jnp.arange(Q_BLOCK)) // CHUNK
            mask = k_chunk[None, :] <= q_chunk[:, None]
            return diff_core(qi, k, v, mask, lam)

        o = lax.map(blk, (qb, jnp.arange(nb)))
        o = jnp.moveaxis(o, 0, 1).reshape(B_, T_, N_HEADS, D_VHEAD)
    else:
        k_all = jnp.concatenate([k_past, k], axis=1)
        v_all = jnp.concatenate([v_past, v], axis=1)
        o = diff_core(q, k_all, v_all, None, lam)
    o = rms_norm(o, p['subln_g']) * (1.0 - lam_init)
    return o.reshape(B_, T_, D_ATTN), k, v

def conv_branch(z, conv_hist, p):
    glu = z[..., OFF_GLU_A:OFF_GLU_B] * jax.nn.sigmoid(z[..., OFF_GLU_B:OFF_Q])
    u = jnp.concatenate([conv_hist.astype(glu.dtype), glu], axis=1)
    w = p['conv_dw_w'].reshape(CONV_WIDTH, 1, D_CONV).astype(u.dtype)
    c = lax.conv_general_dilated(u, w, window_strides=(1,), padding='VALID',
                                 dimension_numbers=('NWC', 'WIO', 'NWC'),
                                 feature_group_count=D_CONV)
    c = c + p['conv_dw_b']
    c = layer_norm(c, p['conv_ln_g'], p['conv_ln_b'])
    c = c * jax.nn.sigmoid(c)
    return c @ p['w_conv_out'], u[:, -CONV_STATE:]

def peer(h, w_pq, sub_k1, sub_k2, u_tab, v_tab):
    B_, T_, D = h.shape
    flat = h.reshape(-1, D)
    n = flat.shape[0]
    nblk = -(-n // PEER_BLOCK)
    flat = jnp.pad(flat, ((0, nblk * PEER_BLOCK - n), (0, 0)))
    f32 = jnp.float32
    half = PEER_DKEY // 2

    def blk(xb):
        q = (xb @ w_pq).reshape(PEER_BLOCK, PEER_HEADS, PEER_DKEY).astype(f32)
        s1 = jnp.einsum('thd,nd->thn', q[..., :half], sub_k1.astype(f32))
        s2 = jnp.einsum('thd,nd->thn', q[..., half:], sub_k2.astype(f32))
        v1, i1 = lax.top_k(s1, PEER_TOPK)
        v2, i2 = lax.top_k(s2, PEER_TOPK)
        cand = (v1[..., :, None] + v2[..., None, :]).reshape(PEER_BLOCK, PEER_HEADS, PEER_TOPK * PEER_TOPK)
        cidx = (i1[..., :, None] * PEER_NKEYS + i2[..., None, :]).reshape(PEER_BLOCK, PEER_HEADS, PEER_TOPK * PEER_TOPK)
        sc, j = lax.top_k(cand, PEER_TOPK)
        idx = jnp.take_along_axis(cidx, j, axis=-1)
        g = jax.nn.softmax(sc, axis=-1)
        ue = u_tab[idx]
        ve = v_tab[idx]
        a = jnp.einsum('td,thkd->thk', xb, ue).astype(f32)
        wgt = (g * jax.nn.gelu(a, approximate=False)).astype(xb.dtype)
        return jnp.einsum('thk,thkd->td', wgt, ve)

    out = lax.map(blk, flat.reshape(nblk, PEER_BLOCK, D))
    return out.reshape(-1, D)[:n].reshape(B_, T_, D)

def layer(x, pos, conv_hist, k_past, v_past, p, lam_init):
    h = rms_norm(x, p['norm1_g'])
    z = h @ p['w_in']
    conv_out, conv_state = conv_branch(z, conv_hist, p)
    attn_o, k_new, v_new = attn_branch(z, pos, k_past, v_past, p, lam_init)
    attn_out = attn_o @ p['w_attn_out']
    merged = (jax.nn.sigmoid(z[..., OFF_GATE_C:OFF_GATE_A]) * conv_out
              + jax.nn.sigmoid(z[..., OFF_GATE_A:D_IN_PROJ]) * attn_out)
    x = x + merged @ p['w_out']
    h2 = rms_norm(x, p['norm2_g'])
    x = x + peer(h2, p['peer_wq'], p['peer_k1'], p['peer_k2'], p['peer_u'], p['peer_v'])
    return x, k_new, v_new, conv_state

def setup_inputs(seed: int = 0) -> dict:
    key = jax.random.key(seed)
    ks = jax.random.split(key, 32)
    nrm = jax.random.normal
    f = jnp.float32
    L = DEPTH
    return {
        'x_prompt': nrm(ks[0], (BATCH, SEQ, D_MODEL), f),
        'x_sample': nrm(ks[1], (DEC_BATCH, DEC_SEQ, D_MODEL), f),
        'cache_attn_k': nrm(ks[2], (L, DEC_BATCH, PAST_LEN, N_HEADS, 2, D_HEAD), f),
        'cache_attn_v': nrm(ks[3], (L, DEC_BATCH, PAST_LEN, N_HEADS, D_VHEAD), f),
        'state_conv': nrm(ks[4], (L, DEC_BATCH, CONV_STATE, D_CONV), f) * 0.5,
        'norm1_g': 1.0 + 0.02 * nrm(ks[5], (L, D_MODEL), f),
        'w_in': nrm(ks[6], (L, D_MODEL, D_IN_PROJ), f) * D_MODEL ** -0.5,
        'conv_dw_w': nrm(ks[7], (L, CONV_WIDTH, D_CONV), f) * CONV_WIDTH ** -0.5,
        'conv_dw_b': 0.02 * nrm(ks[8], (L, D_CONV), f),
        'conv_ln_g': 1.0 + 0.02 * nrm(ks[9], (L, D_CONV), f),
        'conv_ln_b': 0.02 * nrm(ks[10], (L, D_CONV), f),
        'w_conv_out': nrm(ks[11], (L, D_CONV, D_MODEL), f) * D_CONV ** -0.5,
        'q_norm_g': 1.0 + 0.02 * nrm(ks[12], (L, D_HEAD), f),
        'k_norm_g': 1.0 + 0.02 * nrm(ks[13], (L, D_HEAD), f),
        'lambda_q1': 0.1 * nrm(ks[14], (L, D_HEAD), f),
        'lambda_k1': 0.1 * nrm(ks[15], (L, D_HEAD), f),
        'lambda_q2': 0.1 * nrm(ks[16], (L, D_HEAD), f),
        'lambda_k2': 0.1 * nrm(ks[17], (L, D_HEAD), f),
        'subln_g': 1.0 + 0.02 * nrm(ks[18], (L, D_VHEAD), f),
        'w_attn_out': nrm(ks[19], (L, D_ATTN, D_MODEL), f) * D_ATTN ** -0.5,
        'w_out': nrm(ks[20], (L, D_MODEL, D_MODEL), f) * D_MODEL ** -0.5,
        'norm2_g': 1.0 + 0.02 * nrm(ks[21], (L, D_MODEL), f),
        'peer_wq': nrm(ks[22], (L, D_MODEL, PEER_HEADS * PEER_DKEY), f) * D_MODEL ** -0.5,
        'peer_k1': nrm(ks[23], (L, PEER_NKEYS, PEER_DKEY // 2), f) * (PEER_DKEY // 2) ** -0.5,
        'peer_k2': nrm(ks[24], (L, PEER_NKEYS, PEER_DKEY // 2), f) * (PEER_DKEY // 2) ** -0.5,
        'peer_u': nrm(ks[25], (L, PEER_EXPERTS, D_MODEL), f) * D_MODEL ** -0.5,
        'peer_v': nrm(ks[26], (L, PEER_EXPERTS, D_MODEL), f) * 0.5,
    }

def reference(x_prompt, x_sample, cache_attn_k, cache_attn_v, state_conv,
              norm1_g, w_in, conv_dw_w, conv_dw_b, conv_ln_g, conv_ln_b, w_conv_out,
              q_norm_g, k_norm_g, lambda_q1, lambda_k1, lambda_q2, lambda_k2, subln_g,
              w_attn_out, w_out, norm2_g, peer_wq, peer_k1, peer_k2, peer_u, peer_v):
    pos_p = jnp.arange(x_prompt.shape[1])
    pos_s = x_sample.shape[1] * 0 + PAST_LEN + jnp.arange(x_sample.shape[1])
    xp, xs = x_prompt, x_sample
    kp_l, vp_l, cp_l, ksl, vsl, csl = [], [], [], [], [], []
    for l in range(DEPTH):
        p = dict(norm1_g=norm1_g[l], w_in=w_in[l], conv_dw_w=conv_dw_w[l], conv_dw_b=conv_dw_b[l],
                 conv_ln_g=conv_ln_g[l], conv_ln_b=conv_ln_b[l], w_conv_out=w_conv_out[l],
                 q_norm_g=q_norm_g[l], k_norm_g=k_norm_g[l], lambda_q1=lambda_q1[l],
                 lambda_k1=lambda_k1[l], lambda_q2=lambda_q2[l], lambda_k2=lambda_k2[l],
                 subln_g=subln_g[l], w_attn_out=w_attn_out[l], w_out=w_out[l], norm2_g=norm2_g[l],
                 peer_wq=peer_wq[l], peer_k1=peer_k1[l], peer_k2=peer_k2[l],
                 peer_u=peer_u[l], peer_v=peer_v[l])
        li = lambda_init(l)
        zero_hist = jnp.zeros((xp.shape[0], CONV_STATE, D_CONV), xp.dtype)
        xp, kp, vp, cp = layer(xp, pos_p, zero_hist, None, None, p, li)
        xs, ks_, vs_, cs_ = layer(xs, pos_s, state_conv[l], cache_attn_k[l], cache_attn_v[l], p, li)
        kp_l.append(kp); vp_l.append(vp); cp_l.append(cp)
        ksl.append(ks_); vsl.append(vs_); csl.append(cs_)
    k_prompt = jnp.stack(kp_l); v_prompt = jnp.stack(vp_l); conv_prompt = jnp.stack(cp_l)
    k_sample = jnp.stack(ksl); v_sample = jnp.stack(vsl); conv_sample = jnp.stack(csl)
    return (xp, xs, k_prompt, v_prompt, conv_prompt, k_sample, v_sample, conv_sample)


_drawn_inputs = setup_inputs


def setup_inputs(seed=0):
    import zlib

    import numpy as np

    out = dict(_drawn_inputs(seed))
    spreads = {}
    factors = {'conv_ln_g': 7.93,
     'conv_ln_b': 8.538,
     'lambda_q1': 3.953,
     'subln_g': 2.691,
     'q_norm_g': 2.923,
     'k_norm_g': 2.78,
     'norm2_g': 2.754}
    for name, (base, spread) in spreads.items():
        noise = np.random.default_rng([zlib.crc32(name.encode()), seed]).standard_normal(out[name].shape)
        drawn = base * np.exp(spread * noise) if base else spread * noise
        out[name] = __import__('jax').numpy.asarray(drawn.astype(out[name].dtype))
    for name, factor in factors.items():
        out[name] = (out[name] * factor).astype(out[name].dtype)
    return out
```

```python
import numpy as np
import concourse.bass as bass
from concourse import mybir
from concourse.alu_op_type import AluOpType as ALU
from contextlib import ExitStack

F32 = mybir.dt.float32
F32R = mybir.dt.float32r
U32 = mybir.dt.uint32
ACT = mybir.ActivationFunctionType
AX = mybir.AxisListType

P = 128
TP, TS = 512, 32
T = TP + TS
HT = T // 2
PAST = 256
DM = 2048
NH = 8
DH = 64
KD = DM // P
KC = 8
TAPS = 31
HIST = TAPS - 1
CHUNK = 64
EPS = 1e-6
LAM0 = 0.8 - 0.6
TOPK = 16
NKEY = 128
UNITW = 2048
NZ, NA, NC_, NO, NQ, NU, NV = 72, 8, 8, 16, 8, 128, 128
U_ATT = NZ
U_OUT = NZ + NA + NC_
U_PQ = U_OUT + NO
U_PU = U_PQ + NQ
U_PV = U_PU + NU
UNITS = U_PV + NV
ZPH = 9
QT = TP // P
STEPS = QT + 1
GRP = 8
NGRP = NKEY // GRP
GB = 16
NGB = T // GB
TOPK_UNITS = 6
TT = 5
LN_PIECE = 4

C_COS, C_SIN, C_ID, C_BLK, C_PERM, C_ONES, C_NEG, C_END = np.cumsum([0, TP, TP, P, P, P, P, 64]).tolist()
L_IOTA, L_IOTA16, L_BLK16, L_END = np.cumsum([0, P, 16, P]).tolist()
(P_G1, P_G2, P_CW, P_CB, P_LG, P_LB, P_QG, P_KG, P_SUB, P_END) = np.cumsum(
    [0, KD, KD, NH * TAPS, NH, NH, NH, 1, 1, 1]).tolist()
S_EPS, S_NLAM, S_SUB, S_MX, S_NM, S_SUM, S_RC, S_C1, S_L, S_END = 0, 1, 2, 4, 6, 8, 10, 12, 14, 18


class Count:

    def __init__(self, sem):
        self.sem, self.base, self.n, self.trip = sem, 0, 0, None

    def by(self, ins, k=1):
        self.n += k
        return ins.then_inc(self.sem, k)

    def value(self):
        return self.base + self.n

    def loop(self, i, per):
        self.outer = self.base + self.n
        self.base, self.n, self.trip = i * per + self.outer, 0, per

    def endloop(self, rounds):
        assert self.n == self.trip, (self.n, self.trip)
        self.base, self.n = self.outer + rounds * self.trip, 0


def build(nc, w_all, x_t, consts, late, params, lams, keys_t, past_k, past_v, hist,
          y_t, k_t, v_n, cst_p, cst_s):
    ctx = ExitStack()
    with ctx:
        base = (nc.sbuf_base + 31) // 32 * 32
        top = nc.sbuf_usable_end

        class Area:
            def __init__(self, at, size):
                self.at, self.end = at, at + size

            def take(self, name, shape, dt=F32):
                n = int(np.prod(shape[1:])) * 4
                assert self.at + n <= self.end, (name, self.at + n - self.end)
                t = nc.alloc_sbuf_tensor_at(name, shape, dt, offset=self.at)
                self.at += (n + 31) // 32 * 32
                return t

        BIG = 2 * KD * T * 4
        HALF = BIG // 2
        X0, Y0 = base, base + BIG
        W0 = Y0 + BIG
        M0 = W0 + 6 * UNITW * 4
        wa = Area(W0, 6 * UNITW * 4)
        raw = wa.take("w_raw", [P, 2, UNITW])
        w_hi = wa.take("w_hi", [P, 2, UNITW], F32R)
        w_lo = wa.take("w_lo", [P, 2, UNITW], F32R)
        misc = Area(M0, top - M0)
        cst = misc.take("consts_sb", [P, C_END])
        par = misc.take("params_sb", [P, P_END])
        sm = misc.take("small", [P, S_END])
        MT = misc.at
        MEND = top

        ax = Area(X0, BIG)
        h_hi = ax.take("h_hi", [P, KD, T], F32R)
        h_lo = ax.take("h_lo", [P, KD, T], F32R)
        ay = Area(Y0, BIG)
        o_hi = ay.take("o_hi", [P, KC, T], F32R)
        o_lo = ay.take("o_lo", [P, KC, T], F32R)
        c_all = ay.take("c_all", [P, KC, T])
        zb = ay.take("zb", [P, 2, T])
        xg = ay.take("xg", [P, T])
        sq = ay.take("sq", [P, T])
        rstd = ay.take("rstd", [P, T])
        q_t = ay.take("q_t", [P, T])
        kn_t = ay.take("kn_t", [P, T])
        oraw = ay.take("oraw", [P, T])
        az = Area(MT, MEND - MT)
        v_tok = az.take("v_tok", [P, QT, P])
        v_smp = az.take("v_smp", [P, P])
        pk = az.take("pk", [P, PAST])
        pv = az.take("pv", [P, PAST // P, P])
        e = az.take("e", [P, 2, TP])
        a_t = az.take("a_t", [P, TP])
        u = az.take("u", [P, HIST + TP + HIST + TS])
        rs1 = az.take("rs1", [P, T])
        xs = Area(Y0, HALF).take("xs", [P, KD, T])
        a0 = Area(Y0 + HALF, HALF)
        xsq = a0.take("xsq", [P, 2, T])
        xsum = a0.take("xsum", [P, T])
        lam_sb = a0.take("lam_sb", [P, 4, DH])

        am = Area(X0, BIG)
        c_hi = am.take("c_hi", [P, KC, T], F32R)
        c_lo = am.take("c_lo", [P, KC, T], F32R)
        m1 = am.take("m1", [P, KD, T])
        an = Area(Y0, BIG)
        m_hi = an.take("m_hi", [P, KD, T], F32R)
        m_lo = an.take("m_lo", [P, KD, T], F32R)
        ap_ = Area(MT, MEND - MT)
        csq = ap_.take("csq", [P, T])
        ctmp = ap_.take("ctmp", [P, T])
        ly = ap_.take("ly", [P, T])
        lt = ap_.take("lt", [P, T])
        lnr = ap_.take("lnr", [P, T])
        gt = ap_.take("gt", [P, 2, T])
        ao = Area(X0, BIG)
        h2_hi = ao.take("h2_hi", [P, KD, T], F32R)
        h2_lo = ao.take("h2_lo", [P, KD, T], F32R)
        aq = Area(MT, MEND - MT)
        rs2 = aq.take("rs2", [P, T])
        x2 = aq.take("x2", [P, 2, T])
        xt = aq.take("xt", [P, 2, T])
        osq = aq.take("osq", [P, T])
        osum = aq.take("osum", [P, T])
        au = Area(MT, MEND - MT)
        au.take("rs2_again", [P, T])
        ab = au.take("ab", [P, 2, T])
        gb = au.take("gb", [P, 2, T])
        ag = Area(Y0, BIG)
        qp = ag.take("qp", [P, NH, T])
        e_t = ag.take("e_t", [P, T])
        g_hi = ag.take("g_hi", [P, T], F32R)
        i1_t = ag.take("i1_t", [P, T])
        i2_t = ag.take("i2_t", [P, T])
        ksb = ag.take("ksb", [P, NKEY])
        late_sb = ag.take("late_sb", [P, L_END])
        GO = ag.at
        ak = Area(GO, Y0 + BIG - GO)
        sc = ak.take("sc", [P, 2, NH, NKEY])
        wk = ak.take("wk", [P, 2 * NH * NKEY])
        cand = ak.take("cand", [P, NH, TOPK * TOPK])
        tv = ak.take("tv", [P, 2, NH, TOPK])
        ti = ak.take("ti", [P, 2, NH, TOPK], U32)
        tif = ak.take("tif", [P, 2, NH * TOPK])
        sel = ak.take("sel", [P, NH, TOPK])
        ju = ak.take("ju", [P, NH * TOPK], U32)
        jab = ak.take("jab", [P, 2, NH * TOPK], U32)
        jf = ak.take("jf", [P, 2, NH * TOPK])
        ssub = ak.take("ssub", [P, NH * TOPK])
        isel = ak.take("isel", [P, 2, NH * TOPK])
        aw = Area(GO, Y0 + BIG - GO)
        g_st = aw.take("g_st", [P, 2, NKEY, GB])
        oh2 = aw.take("oh2", [P, 8, NKEY], F32R)
        oh1h = aw.take("oh1h", [P, 8, NKEY], F32R)
        oh1l = aw.take("oh1l", [P, 8, NKEY], F32R)
        av = Area(X0, BIG)
        wt_hi = av.take("wt_hi", [P, 2, GRP, T], F32R)
        wt_lo = av.take("wt_lo", [P, 2, GRP, T], F32R)
        avy = Area(Y0, BIG)
        acc = avy.take("acc", [P, KD, T])
        a_st = avy.take("a_st", [P, GRP, T])
        gl_st = avy.take("gl_st", [P, NGB, GRP, GB])

        pair = [ctx.enter_context(nc.psum_tensor(f"pair{i}", [P, 2, 512], F32)) for i in range(2)]
        S = ctx.enter_context(nc.psum_tensor("S", [P, 2, 512], F32))
        TO = ctx.enter_context(nc.psum_tensor("TO", [P, 2, 512], F32))
        PV = [p[:, :, 0:HT] for p in pair]
        SV, TOV = S[:, :, 0:HT], TO[:, :, 0:HT]

        def two(ap):
            return ap.rearrange("p (a b) -> p a b", a=2)

        gate_scr = nc.dram_tensor("gate_scr", (2 * KD, P, T), F32, kind="Internal").ap()
        x2_scr = nc.dram_tensor("x2_scr", (KD, P, T), F32, kind="Internal").ap()
        a_scr = nc.dram_tensor("a_scr", (NKEY, P, T), F32, kind="Internal").ap()
        g_scr = nc.dram_tensor("g_scr", (NGB, P, NKEY, GB), F32, kind="Internal").ap()

        def sem(name):
            return ctx.enter_context(nc.semaphore(name))

        w_loaded = [sem("w_loaded0"), sem("w_loaded1")]
        hi_ready, lo_ready = sem("hi_ready"), sem("lo_ready")
        unit_done = sem("unit_done")
        tile_done = sem("tile_done")
        dve_step, act_step = sem("dve_step"), sem("act_step")
        const_loaded, late_loaded = sem("const_loaded"), sem("late_loaded")
        x_loaded = [sem(f"x_loaded{i}") for i in range(4)]
        xsq_added = sem("xsq_added")
        xhi_ready, xlo_ready, lam_ready, u_zeroed = sem("xhi_ready"), sem("xlo_ready"), sem("lam_ready"), sem("u_zeroed")
        zb_full, z_taken = sem("zb_full"), sem("z_taken")
        sq_ready, stat_ready, std_ready = sem("sq_ready"), sem("stat_ready"), sem("std_ready")
        rot_ready, rot_taken, norm_done = sem("rot_ready"), sem("rot_taken"), sem("norm_done")
        vt_ready, v_ready = sem("vt_ready"), sem("v_ready")
        k_stored, v_stored, gate_stored = sem("k_stored"), sem("v_stored"), [sem("gate_stored0"), sem("gate_stored1")]
        past_loaded, hist_loaded, glu_ready, conv_done, cstate_stored = (
            sem("past_loaded"), sem("hist_loaded"), sem("glu_ready"), sem("conv_done"), sem("cstate_stored"))
        sc_ready, nmax_ready, exp_done, a_ready = sem("sc_ready"), sem("nmax_ready"), sem("exp_done"), sem("a_ready")
        tr_ready, at_ready, av_ready, o_ready = sem("tr_ready"), sem("at_ready"), sem("av_ready"), sem("o_ready")
        mean_ready, csq_ready, var_ready, lnstd_ready = (
            sem("mean_ready"), sem("csq_ready"), sem("var_ready"), sem("lnstd_ready"))
        ly_ready, lt_ready, cn_ready = sem("ly_ready"), sem("lt_ready"), sem("cn_ready")
        gt_loaded = [sem("gt_loaded0"), sem("gt_loaded1")]
        m_taken, merged_ready = sem("m_taken"), sem("merged_ready")
        xt_loaded = [sem("xt_loaded0"), sem("xt_loaded1")]
        x2_ready, x2_stored, h2_ready = sem("x2_ready"), [sem("x2_stored0"), sem("x2_stored1")], sem("h2_ready")
        osum_ready, ostat_ready, ostd_ready, rs2_ready, qp_ready = (
            sem("osum_ready"), sem("ostat_ready"), sem("ostd_ready"), sem("rs2_ready"), sem("qp_ready"))
        ab_full, ab_scaled, gelu_done = sem("ab_full"), sem("ab_scaled"), sem("gelu_done")
        a_stored = [sem("a_stored0"), sem("a_stored1")]
        scores_ready, scores_taken, chosen, chosen_t, chosen_taken = (
            sem("scores_ready"), sem("scores_taken"), sem("chosen"), sem("chosen_t"), sem("chosen_taken"))
        gsum_ready = sem("gsum_ready")
        oh_ready, grp_done, grp_taken = sem("oh_ready"), sem("grp_done"), sem("grp_taken")
        g_stored = [sem("g_stored0"), sem("g_stored1")]
        acc_loaded, al_loaded, gl_loaded, w_prepped = sem("acc_loaded"), sem("al_loaded"), sem("gl_loaded"), sem("w_prepped")
        acc_added, y_stored = sem("acc_added"), sem("y_stored")

        block = ctx.enter_context(nc.Block())

        @block.sync
        def _(sp):
            def load_w(pairno, slot):
                sp.dma_start(raw[:, slot, :], w_all[bass.ds(pairno * 2 + slot, 1)].rearrange("a p n -> p (a n)"))\
                    .then_inc(w_loaded[slot], 16)

            for s in (av_ready, conv_done, cstate_stored, norm_done, v_stored, tr_ready, exp_done, k_stored, sc_ready,
                      o_ready, at_ready, *gate_stored, *a_stored, *g_stored, *x2_stored):
                sp.sem_inc(s, 1)
            for i in range(4):
                sp.dma_start(xs[:, 4 * i:4 * i + 4, :], x_t[:, 4 * i:4 * i + 4, :]).then_inc(x_loaded[i], 16)
                if i in (0, 1):
                    load_w(0, i)

            def z_loads(hp, last):
                for r in range(2):
                    h = hp * 2 + r
                    for i in range(ZPH):
                        n = r * ZPH + i
                        sp.wait_ge(lo_ready, hp * (2 * ZPH) + (n + 1))
                        load_w(hp * ZPH + (n // 2 + 1), n % 2)
                        if i == 1:
                            sp.wait_ge(av_ready, h * STEPS + 1)
                            sp.dma_start(pk[:, :], past_k[bass.ds(h, 1)].rearrange("a p n -> p (a n)"))\
                                .then_inc(past_loaded, 16)
                            sp.wait_ge(cstate_stored, h * 32 + 1)
                            sp.dma_start(pv[:, :, :], past_v[bass.ds(h, 1)].rearrange("a p b n -> p (a b) n"))\
                                .then_inc(past_loaded, 16)
                        if i == 2:
                            sp.wait_ge(conv_done, h + 1)
                            sp.dma_start(u[:, HIST + TP:HIST + TP + HIST],
                                         hist[bass.ds(h, 1)].rearrange("a p n -> p (a n)")).then_inc(hist_loaded, 16)
                        if i == 5:
                            sp.wait_ge(norm_done, h * 3 + 2 + 1)
                            sp.dma_start(k_t[bass.ds(h, 1)].rearrange("a p n -> p (a n)"), kn_t[:, :])\
                                .then_inc(k_stored, 16)
                            sp.wait_ge(v_ready, h + 1)
                            sp.dma_start(v_n[0:TP, bass.ds(h, 1), :].rearrange("(b p) a n -> p b (a n)", p=P), v_tok[:, :, :])\
                                .then_inc(v_stored, 16)
                            sp.dma_start(v_n[TP:T, bass.ds(h, 1), :].rearrange("p a n -> p (a n)"), v_smp[0:TS, :])\
                                .then_inc(v_stored, 16)
                        if i == 7:
                            sp.wait_ge(glu_ready, h + 1)
                            sp.dma_start(cst_p[bass.ds(h, 1)].rearrange("a p n -> p (a n)"), u[:, TP:TP + HIST])\
                                .then_inc(cstate_stored, 16)
                            o = HIST + TP + TS
                            sp.dma_start(cst_s[bass.ds(h, 1)].rearrange("a p n -> p (a n)"), u[:, o:o + HIST])\
                                .then_inc(cstate_stored, 16)

            with sp.Fori(0, NH // 2) as hp:
                z_loads(hp, False)

            sp.wait_ge(gate_stored[0], 16 * 2 * NH + 1)
            sp.wait_ge(gate_stored[1], 16 * 2 * NH + 1)
            sp.wait_ge(av_ready, NH * STEPS + 1)
            sp.wait_ge(conv_done, NH + 1)
            sp.wait_ge(cstate_stored, 32 * NH + 1)
            sp.wait_ge(v_stored, 32 * NH + 1)

            def merge_loads(v, gate0, tile0):
                for n in range(2):
                    sp.wait_ge(lo_ready, v * 2 + (n + 1 + NZ + tile0 // 2))
                    load_w(v + ((NZ + tile0 // 2) // 2 + 1), n)
                    for k in range(2):
                        ct = v * 4 + (2 * n + k)
                        sp.wait_ge(m_taken, ct + (tile0 + 1))
                        sp.dma_start(gt[:, k, :], gate_scr[bass.ds(ct + gate0, 1)].rearrange("a p n -> p (a n)"))\
                            .then_inc(gt_loaded[k], 16)

            with sp.Fori(0, NA // 2) as v:
                merge_loads(v, KD, 0)
            with sp.Fori(0, NC_ // 2) as v:
                merge_loads(v, 0, KD)

            sp.wait_ge(m_taken, 2 + 2 * KD)
            with sp.Fori(0, NO // 2) as v:
                for n in range(2):
                    sp.wait_ge(lo_ready, v * 2 + (n + 1 + U_OUT))
                    load_w(v + (U_OUT // 2 + 1), n)
                    sp.wait_ge(x2_ready, v * 2 + (n + 1))
                    sp.dma_start(xt[:, n, :], x_t[:, bass.ds(v * 2 + n, 1), :].rearrange("p a n -> p (a n)"))\
                        .then_inc(xt_loaded[n], 16)
            sp.wait_ge(unit_done, NZ + NO)
            sp.dma_start(ksb[:, :], keys_t).then_inc(late_loaded, 16)
            sp.dma_start(late_sb[:, :], late).then_inc(late_loaded, 16)
            with sp.Fori(0, (NQ + NU) // 2) as v:
                for n in range(2):
                    sp.wait_ge(lo_ready, v * 2 + (n + 1 + U_PQ))
                    load_w(v + (U_PQ // 2 + 1), n)

            for s in a_stored:
                sp.wait_ge(s, 16 * NU // 2 + 1)
            for s in g_stored:
                sp.wait_ge(s, 16 * NGB // 2 + 1)
            for s in x2_stored:
                sp.wait_ge(s, 16 * KD // 2 + 1)
            sp.wait_ge(oh_ready, NGB * 4)
            sp.wait_ge(grp_done, 2 + NGB * 4)

            def load_ag(g):
                sp.dma_start(a_st[:, :, :], a_scr[bass.ds(g * GRP, GRP)].rearrange("c p n -> p c n")).then_inc(al_loaded, 16)
                sp.dma_start(gl_st[:, :, :, :].rearrange("p b c n -> p b (c n)"),
                             g_scr[:, :, bass.ds(g * GRP, GRP), :].rearrange("b p c n -> p b (c n)"))\
                    .then_inc(gl_loaded, 16)

            load_ag(0)
            sp.dma_start(acc[:, :, :], x2_scr.rearrange("c p n -> p c n")).then_inc(acc_loaded, 16)
            sp.wait_ge(w_prepped, GRP)
            load_ag(1)
            with sp.Fori(0, NGRP - 2) as g:
                for n in range(GRP):
                    sp.wait_ge(lo_ready, g * GRP + (n + 1 + U_PV))
                    load_w(g * (GRP // 2) + (U_PV // 2 + 1 + n // 2), n % 2)
                sp.wait_ge(w_prepped, g * GRP + 2 * GRP)
                load_ag(g + 2)
            for n in range(2 * GRP - 2):
                sp.wait_ge(lo_ready, (NGRP - 2) * GRP + n + 1 + U_PV)
                load_w((NGRP - 2) * (GRP // 2) + U_PV // 2 + 1 + n // 2, n % 2)
            for d in range(KD):
                sp.wait_ge(acc_added, 2 + (NGRP - 1) * KD + d + 1)
                sp.dma_start(y_t[d], acc[:, d, :]).then_inc(y_stored, 16)
            sp.wait_ge(y_stored, 16 * KD)
            sp.wait_ge(k_stored, 16 * NH + 1)

        @block.gpsimd
        def _(pool):
            pool.memset(u[:, 0:HIST], 0.0).then_inc(u_zeroed, 1)

            def lo(w, slot):
                pool.wait_ge(hi_ready, w + 1)
                pool.tensor_tensor(w_lo[:, slot, :], raw[:, slot, :], w_hi[:, slot, :].bitcast(F32), ALU.subtract)\
                    .then_inc(lo_ready, 1)

            with pool.Fori(0, U_PU // 2 + 1) as v:
                for n in range(2):
                    lo(v * 2 + n, n)
            pool.wait_ge(rs2_ready, 1)
            with pool.Fori(0, NU // 2) as v:
                for n in range(2):
                    pool.wait_ge(ab_full, v * 2 + (n + 1 + 2))
                    pool.tensor_tensor(ab[:, n, :], ab[:, n, :], rs2[:, :], ALU.mult).then_inc(ab_scaled, 1)
                    lo(v * 2 + (n + U_PU + 2), n)
            with pool.Fori(0, NV // 2 - 1) as v:
                for n in range(2):
                    lo(v * 2 + (n + U_PV + 2), n)

        @block.scalar
        def _(act):
            own = Count(act_step)
            for dst, src in ((cst, consts), (par, params)):
                act.dma_start(dst[:, :], src).then_inc(const_loaded, 16)
            act.dma_start(lam_sb[:, :, :], lams).then_inc(const_loaded, 16)
            act.sem_inc(ab_full, 2)

            def hi(pairno, slot):
                act.wait_ge(w_loaded[slot], pairno * 16 + 16)
                act.activation(w_hi[:, slot, :], raw[:, slot, :], ACT.Copy).then_inc(hi_ready, 1)

            act.wait_ge(const_loaded, 48)
            for k in range(KD):
                act.wait_ge(x_loaded[k // 4], 16)
                if k >= 2:
                    act.wait_ge(xsq_added, k - 1)
                act.activation(xsq[:, k % 2, :], xs[:, k, :], ACT.Square)
                act.activation(h_hi[:, k, :], xs[:, k, :], ACT.Copy, scale=par[:, P_G1 + k:P_G1 + k + 1])\
                    .then_inc(xhi_ready, 1)
                if k in (4, 8):
                    hi(0, k // 4 - 1)
            act.wait_ge(stat_ready, 1)
            act.activation(rs1[:, :], SV, ACT.Sqrt, scale=1.0 / DM, bias=sm[:, S_EPS:S_EPS + 1]).then_inc(std_ready, 1)
            act.wait_ge(lam_ready, 1)
            act.activation(sm[:, S_L + 2:S_L + 4], sm[:, S_L:S_L + 2], ACT.Exp).then_inc(std_ready, 1)

            def std(inv_n):
                act.activation(rstd[:, :], SV, ACT.Sqrt, scale=inv_n, bias=sm[:, S_EPS:S_EPS + 1]).then_inc(std_ready, 1)

            def z_slot(hp, r, i):
                h = hp * 2 + r
                n = r * ZPH + i
                j = n % 2
                un = hp * (2 * ZPH) + n
                act.wait_ge(zb_full, un + 3)
                if i in (0, 1):
                    m = h * 3 + i
                    act.wait_ge(norm_done, m + 1)
                    act.wait_ge(conv_done, h + 1)
                    act.activation(sq[:, :], zb[:, j, :], ACT.Square).then_inc(sq_ready, 1)
                    act.activation(xg[:, :], zb[:, j, :], ACT.Copy, scale=par[:, P_QG + i:P_QG + i + 1]).then_inc(z_taken, 1)
                if i >= 4:
                    act.activation(zb[:, j, :], zb[:, j, :], ACT.Tanh, scale=0.5).then_inc(z_taken, 1)
                if i >= 5:
                    act.wait_ge(z_taken, h * 7 + (i - 1))
                    act.dma_start(gate_scr[bass.ds(h * 2 + ((i - 5) if i < 7 else (KD + i - 7)), 1)].rearrange("a p n -> p (a n)"),
                                  zb[:, j, :]).then_inc(gate_stored[(i - 5) % 2], 16)
                act.wait_ge(unit_done, un + 1)
                hi(hp * ZPH + (n // 2 + 1), j)
                if i in (0, 1):
                    act.wait_ge(stat_ready, h * 3 + (i + 2))
                    std(1.0 / DH)

            def values_out(h):
                act.wait_ge(vt_ready, h + 1)
                act.wait_ge(v_stored, h * 32 + 1)
                own.by(act.activation(v_tok[:, :, :].rearrange("p b n -> p (b n)"), TO[:, 0, :], ACT.Copy))
                act.activation(v_smp[0:TS, :], TO[0:TS, 1, 0:P], ACT.Copy).then_inc(v_ready, 1)

            def att_exp(g, i):
                pr = TS if i == QT else P
                keys = PAST + TS if i == QT else (i + 1) * P
                act.wait_ge(nmax_ready, g + 1)
                act.wait_ge(tr_ready, g + 1)
                for c in range(2):
                    ins = act.activation(e[0:pr, c, 0:keys], S[0:pr, c, 0:keys], ACT.Exp, scale=DH ** -0.5,
                                         bias=sm[0:pr, S_NM + c:S_NM + c + 1], accum_out=sm[0:pr, S_SUM + c:S_SUM + c + 1])
                    (own.by(ins) if c == 0 else ins.then_inc(exp_done, 1))

            def att_at(g, i):
                act.wait_ge(tr_ready, g + 1 + 1)
                act.wait_ge(av_ready, g + 1)
                if i < QT:
                    act.activation(a_t[:, 0:(i + 1) * P], TO[:, 0, 0:(i + 1) * P], ACT.Copy).then_inc(at_ready, 1)
                else:
                    own.by(act.activation(a_t[:, 0:2 * TS], TO[:, 0, 0:2 * TS], ACT.Copy))
                    act.activation(a_t[0:TS, 2 * TS:3 * TS], TO[0:TS, 0, 2 * TS:3 * TS], ACT.Copy).then_inc(at_ready, 1)

            def att_o(h, g, i):
                w = TS if i == QT else P
                act.wait_ge(av_ready, g + 1 + 1)
                if i == 0:
                    act.wait_ge(norm_done, h * 3 + 1)
                act.activation(oraw[:, i * P:i * P + w], TO[:, 1, 0:w], ACT.Copy).then_inc(o_ready, 1)
                if i == QT:
                    act.wait_ge(o_ready, g + 1 + 1)
                    act.wait_ge(norm_done, h * 3 + 2 + 1)
                    act.activation(sq[:, :], oraw[:, :], ACT.Square).then_inc(sq_ready, 1)

            per = 2 * (1 + STEPS + 1)
            with act.Fori(0, NH // 2) as hp:
                own.loop(hp, per)
                for r in range(2):
                    h = hp * 2 + r
                    for i in range(ZPH):
                        s = i - 3
                        g = h * STEPS + s
                        if s > 0:
                            att_o(h, g - 1, s - 1)
                        if 0 <= s < STEPS:
                            att_exp(g, s)
                            if s == 0:
                                values_out(h)
                            att_at(g, s)
                        if s == STEPS:
                            act.wait_ge(stat_ready, h * 3 + 4)
                            std(1.0 / P)
                        z_slot(hp, r, i)
            own.endloop(NH // 2)

            act.wait_ge(unit_done, NZ)

            def merge_hi(v, n, unit0):
                act.wait_ge(tile_done, v * 4 + (2 * n + 2 + 2 * unit0))
                hi(v + ((NZ + unit0) // 2 + 1), n)

            with act.Fori(0, NA // 4) as v:
                for n in range(2):
                    merge_hi(v, n, 0)
            act.wait_ge(var_ready, 1)
            act.activation(lnr[:, :], TOV, ACT.Sqrt, scale=1.0 / (KC * P), bias=sm[:, S_EPS:S_EPS + 1]).then_inc(lnstd_ready, 1)
            with act.Fori(0, NA // 4) as v:
                own.loop(v, 4)
                for n in range(2):
                    for k in range(2):
                        ct = v * 4 + (2 * n + k)
                        act.wait_ge(ly_ready, ct + 1)
                        own.by(act.activation(ly[:, :], ly[:, :], ACT.Identity, scale=par[:, bass.ds(ct + P_LG, 1)],
                                              bias=par[:, bass.ds(ct + P_LB, 1)]))
                        act.wait_ge(act_step, own.value())
                        act.activation(lt[:, :], ly[:, :], ACT.Tanh, scale=0.5).then_inc(lt_ready, 1)
                    merge_hi(v, n, NA // 2)
            own.endloop(NA // 4)
            with act.Fori(0, NC_ // 2) as v:
                for n in range(2):
                    merge_hi(v, n, NA)

            with act.Fori(0, NO // 2) as v:
                for n in range(2):
                    act.wait_ge(x2_ready, v * 2 + (n + 3))
                    act.dma_start(x2_scr[bass.ds(v * 2 + n, 1)].rearrange("a p n -> p (a n)"), x2[:, n, :])\
                        .then_inc(x2_stored[n], 16)
                    act.wait_ge(unit_done, v * 2 + (n + 1 + NZ))
                    hi(v + (U_OUT // 2 + 1), n)
            act.wait_ge(ostat_ready, 1)
            act.activation(rs2[:, :], SV, ACT.Sqrt, scale=1.0 / DM, bias=sm[:, S_EPS:S_EPS + 1]).then_inc(ostd_ready, 1)
            with act.Fori(0, NQ // 2) as v:
                for n in range(2):
                    act.wait_ge(unit_done, v * 2 + (n + 1 + NZ + NO))
                    hi(v + (U_PQ // 2 + 1), n)

            for s in x2_stored:
                act.wait_ge(s, 16 * NO // 2 + 1)

            def u_slot(v, n, groups=None):
                m = v * 2 + n
                act.wait_ge(unit_done, m + (1 + NZ + NO + NQ))
                act.activation(two(ab[:, n, :]), PV[n], ACT.Copy).then_inc(ab_full, 1)
                hi(v + (U_PU // 2 + 1), n)
                if groups:
                    groups()
                act.wait_ge(ab_scaled, m + 1)
                act.wait_ge(a_stored[n], v * 16 + 1)
                act.activation(gb[:, n, :], ab[:, n, :], ACT.Gelu).then_inc(gelu_done, 1)
                act.wait_ge(gelu_done, m + 1)
                act.dma_start(a_scr[bass.ds(m, 1)].rearrange("a p n -> p (a n)"), gb[:, n, :]).then_inc(a_stored[n], 16)

            for s in range(TT):
                with act.Fori(0, TOPK_UNITS // 2) as v:
                    for n in range(2):
                        u_slot(v + s * TOPK_UNITS // 2, n)
                w = TS if s == TT - 1 else P
                act.wait_ge(chosen_t, s + 1)
                own.by(act.activation(e_t[:, s * P:s * P + w], S[:, 0, 0:w], ACT.Exp))
                own.by(act.activation(i1_t[:, s * P:s * P + w], S[:, 0, P:P + w], ACT.Copy))
                act.activation(i2_t[:, s * P:s * P + w], S[:, 0, 2 * P:2 * P + w], ACT.Copy).then_inc(chosen_taken, 1)
            banks = [S[:, 0, :], S[:, 1, :], TO[:, 0, :], TO[:, 1, :]]
            act.sem_inc(grp_taken, 4)
            v0 = TT * TOPK_UNITS // 2
            with act.Fori(0, NGB // 2) as v:
                for b in range(2):
                    for n in range(2):
                        def groups():
                            for q in range(2):
                                gg = v * 8 + (4 * b + 2 * n + q)
                                act.wait_ge(grp_done, gg + 3)
                                if n == 0 and q == 0:
                                    act.wait_ge(g_stored[b], v * 16 + 1)
                                t0 = 8 * n + 4 * q
                                act.activation(g_st[:, b, :, t0:t0 + 4].rearrange("p c t -> p t c"),
                                               banks[2 * n + q].rearrange("p (t c) -> p t c", t=4), ACT.Copy)\
                                    .then_inc(grp_taken, 1)
                        u_slot(v * 2 + (v0 + b), n, groups)
                    act.wait_ge(grp_taken, v * 8 + (4 * b + 4 + 4))
                    act.dma_start(g_scr[bass.ds(v * 2 + b, 1)].rearrange("a p c t -> p (a c t)"),
                                  g_st[:, b, :, :].rearrange("p c t -> p (c t)")).then_inc(g_stored[b], 16)
            v1 = v0 + NGB
            with act.Fori(0, NU // 2 - v1) as v:
                for n in range(2):
                    u_slot(v + v1, n)
            with act.Fori(0, NV // 2 - 1) as v:
                for n in range(2):
                    act.wait_ge(tile_done, v * 4 + (2 * n + 2 + 4 * NA))
                    hi(v + (U_PV // 2 + 1), n)

        @block.vector
        def _(dve):
            V = nc.vector
            own = Count(dve_step)

            def settle():
                dve.wait_ge(dve_step, own.value())

            own.by(V.memset(sm[:, :], EPS))
            own.by(V.memset(xsum[:, :], 0.0))
            dve.wait_ge(const_loaded, 48)
            for k in range(KD):
                dve.wait_ge(xhi_ready, k + 1)
                settle() if k == 0 else dve.wait_ge(xlo_ready, k)
                V.tensor_tensor(xsum[:, :], xsum[:, :], xsq[:, k % 2, :], ALU.add).then_inc(xsq_added, 1)
                V.scalar_tensor_tensor(h_lo[:, k, :], xs[:, k, :], par[:, P_G1 + k:P_G1 + k + 1],
                                       h_hi[:, k, :].bitcast(F32), ALU.mult, ALU.subtract).then_inc(xlo_ready, 1)
            own.by(V.tensor_scalar(sm[:, S_SUB:S_SUB + 1], par[:, P_SUB:P_SUB + 1], 1.0 - LAM0, None, ALU.mult))
            own.by(V.tensor_tensor(lam_sb[:, 0:2, :], lam_sb[:, 0:2, :], lam_sb[:, 2:4, :], ALU.mult))
            settle()
            V.tensor_reduce(sm[:, S_L:S_L + 2], lam_sb[:, 0:2, :], AX.X, ALU.add).then_inc(lam_ready, 1)
            dve.wait_ge(std_ready, 2)
            own.by(V.reciprocal(rs1[:, :], rs1[:, :]))
            own.by(V.tensor_tensor(sm[:, S_NLAM:S_NLAM + 1], sm[:, S_L + 3:S_L + 4], sm[:, S_L + 2:S_L + 3], ALU.subtract))
            settle()
            own.by(V.tensor_scalar(sm[:, S_NLAM:S_NLAM + 1], sm[:, S_NLAM:S_NLAM + 1], -LAM0, None, ALU.add))
            dve.sem_inc(zb_full, 2)
            dve.sem_inc(m_taken, 2)
            dve.sem_inc(x2_ready, 2)
            dve.sem_inc(acc_added, 2)
            settle()

            def evac(hp, r, i):
                h = hp * 2 + r
                j = (r + i) % 2
                dve.wait_ge(unit_done, hp * (2 * ZPH) + (r * ZPH + i + 1))
                if i == 0:
                    dve.wait_ge(gate_stored[0], h * 32 + 1)
                elif i == 1:
                    dve.wait_ge(gate_stored[1], h * 32 + 1)
                elif i in (2, 3):
                    dve.wait_ge(z_taken, h * 7 + (i - 1))
                elif i == 4:
                    dve.wait_ge(vt_ready, h + 1)
                elif i == 5:
                    dve.wait_ge(glu_ready, h + 1)
                elif i == 6:
                    dve.wait_ge(z_taken, h * 7 + 3)
                else:
                    dve.wait_ge(gate_stored[i - 7], h * 32 + 16 + 1)
                if i == 6:
                    dve.wait_ge(glu_ready, h + 1)
                if i == 3:
                    V.scalar_tensor_tensor(two(zb[:, j, :]), PV[j], 0.5, two(rs1[:, :]), ALU.mult, ALU.mult).then_inc(zb_full, 1)
                else:
                    V.tensor_tensor(two(zb[:, j, :]), PV[j], two(rs1[:, :]), ALU.mult).then_inc(zb_full, 1)

            def rope(h, i):
                dve.wait_ge(std_ready, h * 3 + (i + 3))
                own.by(V.reciprocal(rstd[:, :], rstd[:, :]))
                cs = ((slice(0, TP), slice(0, TP)), (slice(TP, T), slice(PAST, PAST + TS)))
                dve.wait_ge(rot_ready, h * 2 + (i + 1))
                for to, fr in cs:
                    own.by(V.tensor_tensor(xg[:, to], xg[:, to], cst[:, fr], ALU.mult))
                s0, t0 = C_SIN, TP - HT
                own.by(V.tensor_tensor(sq[:, 0:HT], TO[:, 0, 0:HT], cst[:, s0:s0 + HT], ALU.mult))
                own.by(V.tensor_tensor(sq[:, HT:TP], TO[:, 1, 0:t0], cst[:, s0 + HT:s0 + TP], ALU.mult))
                V.tensor_tensor(sq[:, TP:T], TO[:, 1, t0:HT], cst[:, s0 + PAST:s0 + PAST + TS], ALU.mult).then_inc(rot_taken, 1)
                dve.wait_ge(rot_taken, h * 2 + (i + 1))
                own.by(V.tensor_tensor(xg[:, :], xg[:, :], sq[:, :], ALU.add))
                settle()
                if i == 0:
                    dve.wait_ge(sc_ready, h * STEPS + 1)
                else:
                    dve.wait_ge(k_stored, h * 16 + 1)
                V.tensor_tensor((kn_t if i else q_t)[:, :], xg[:, :], rstd[:, :], ALU.mult).then_inc(norm_done, 1)

            def att_max(g, i):
                pr = TS if i == QT else P
                keys = PAST + TS if i == QT else (i + 1) * P
                dve.wait_ge(sc_ready, g + 1 + 1)
                own.by(V.tensor_reduce(sm[0:pr, S_MX:S_MX + 2], S[0:pr, :, 0:keys], AX.X, ALU.max))
                settle()
                dve.wait_ge(exp_done, g + 1)
                V.tensor_scalar(sm[0:pr, S_NM:S_NM + 2], sm[0:pr, S_MX:S_MX + 2], -(DH ** -0.5), None, ALU.mult)\
                    .then_inc(nmax_ready, 1)

            def att_mix(g, i):
                pr = TS if i == QT else P
                keys = PAST + TS if i == QT else (i + 1) * P
                dve.wait_ge(exp_done, g + 1 + 1)
                own.by(V.reciprocal(sm[0:pr, S_RC:S_RC + 2], sm[0:pr, S_SUM:S_SUM + 2]))
                settle()
                own.by(V.tensor_scalar(e[0:pr, 0, 0:keys], e[0:pr, 0, 0:keys], sm[0:pr, S_RC:S_RC + 1], None, ALU.mult))
                own.by(V.tensor_tensor(sm[0:pr, S_C1:S_C1 + 1], sm[0:pr, S_RC + 1:S_RC + 2], sm[0:pr, S_NLAM:S_NLAM + 1], ALU.mult))
                settle()
                V.scalar_tensor_tensor(e[0:pr, 0, 0:keys], e[0:pr, 1, 0:keys], sm[0:pr, S_C1:S_C1 + 1],
                                       e[0:pr, 0, 0:keys], ALU.mult, ALU.add).then_inc(a_ready, 1)

            def glu(h, j):
                dve.wait_ge(z_taken, h * 7 + 3)
                dve.wait_ge(hist_loaded, h * 16 + 16)
                a, b = zb[:, 1 - j, :], zb[:, j, :]
                own.by(V.scalar_tensor_tensor(u[:, HIST:HIST + TP], b[:, 0:TP], 1.0, a[:, 0:TP], ALU.add, ALU.mult))
                V.scalar_tensor_tensor(u[:, HIST + TP + HIST:], b[:, TP:T], 1.0, a[:, TP:T], ALU.add, ALU.mult)\
                    .then_inc(glu_ready, 1)

            def taps(h, lo_, hi_):
                for w in range(lo_, hi_):
                    cw = par[:, bass.ds(h * TAPS + (P_CW + w), 1)]
                    segs = ((0, TP, 0), (TP, T, HIST))
                    if w == 0:
                        dve.wait_ge(glu_ready, h + 1)
                    else:
                        settle()
                    for a, b, sh in segs:
                        src = u[:, a + sh + w:b + sh + w]
                        if w == 0:
                            own.by(V.tensor_scalar(xg[:, a:b], src, cw, par[:, bass.ds(h + P_CB, 1)], ALU.mult, ALU.add))
                        elif w < TAPS - 1:
                            own.by(V.scalar_tensor_tensor(xg[:, a:b], src, cw, xg[:, a:b], ALU.mult, ALU.add))
                        else:
                            dst = c_all[:, bass.ds(h, 1), a:b].rearrange("p a n -> p (a n)")
                            ins = V.scalar_tensor_tensor(dst, src, cw, xg[:, a:b], ALU.mult, ALU.add)
                            (own.by(ins) if a == 0 else ins.then_inc(conv_done, 1))

            def o_norm(h):
                dve.wait_ge(std_ready, h * 3 + 5)
                own.by(V.reciprocal(rstd[:, :], rstd[:, :]))
                settle()
                own.by(V.tensor_tensor(oraw[:, :], oraw[:, :], rstd[:, :], ALU.mult))
                settle()
                sub = sm[:, S_SUB:S_SUB + 1]
                ohi = o_hi[:, bass.ds(h, 1), :].rearrange("p a n -> p (a n)")
                own.by(V.tensor_scalar(ohi, oraw[:, :], sub, None, ALU.mult))
                settle()
                V.scalar_tensor_tensor(o_lo[:, bass.ds(h, 1), :].rearrange("p a n -> p (a n)"), oraw[:, :], sub,
                                       ohi.bitcast(F32), ALU.mult, ALU.subtract).then_inc(norm_done, 1)

            per_head = 2 * 6 + 4 * STEPS + 1 + (2 * TAPS - 1) + 3
            with dve.Fori(0, NH // 2) as hp:
                own.loop(hp, 2 * per_head)
                for r in range(2):
                    h = hp * 2 + r
                    g = h * STEPS
                    evac(hp, r, 0)
                    rope(h, 0)
                    evac(hp, r, 1)
                    rope(h, 1)
                    evac(hp, r, 2)
                    for s in range(2):
                        att_max(g + s, s)
                        att_mix(g + s, s)
                        evac(hp, r, s + 3)
                    glu(h, (r + 4) % 2)
                    taps(h, 0, 2)
                    for s in range(2, STEPS):
                        w = 2 + 8 * (s - 2)
                        att_max(g + s, s)
                        taps(h, w, w + 4)
                        att_mix(g + s, s)
                        taps(h, w + 4, w + 6)
                        evac(hp, r, s + 3)
                        taps(h, w + 6, w + 8)
                    taps(h, 2 + 8 * (STEPS - 2), TAPS)
                    o_norm(h)
                    evac(hp, r, 8)
            own.endloop(NH // 2)

            dve.wait_ge(av_ready, NH * STEPS + 1)
            dve.wait_ge(v_stored, NH * 32 + 1)
            dve.wait_ge(cstate_stored, NH * 32 + 1)
            own.by(V.memset(csq[:, :], 0.0))
            settle()

            def att_tile(v, n, k):
                ct = v * 4 + (2 * n + k)
                dve.wait_ge(tile_done, ct + 1)
                dve.wait_ge(gt_loaded[k], v * 32 + (16 * n + 16))
                V.scalar_tensor_tensor(two(m1[:, bass.ds(ct, 1), :].rearrange("p a n -> p (a n)")), two(gt[:, k, :]), 1.0,
                                       PV[k], ALU.add, ALU.mult).then_inc(m_taken, 1)

            dve.wait_ge(mean_ready, 1)
            with dve.Fori(0, NA // 4) as v:
                own.loop(v, 12)
                for n in range(2):
                    for k in range(2):
                        ct = v * 4 + (2 * n + k)
                        att_tile(v, n, k)
                        c = c_all[:, bass.ds(ct, 1), :].rearrange("p a n -> p (a n)")
                        own.by(V.scalar_tensor_tensor(two(c), SV, -1.0 / (KC * P), two(c), ALU.mult, ALU.add))
                        settle()
                        own.by(V.tensor_tensor(ctmp[:, :], c, c, ALU.mult))
                        settle()
                        own.by(V.tensor_tensor(csq[:, :], csq[:, :], ctmp[:, :], ALU.add))
                        settle()
            own.endloop(NA // 4)
            V.tensor_copy(ctmp[:, :], csq[:, :]).then_inc(csq_ready, 1)
            dve.wait_ge(lnstd_ready, 1)
            own.by(V.reciprocal(lnr[:, :], lnr[:, :]))
            settle()
            with dve.Fori(0, NA // 4) as v:
                own.loop(v, 8)
                for n in range(2):
                    for k in range(2):
                        ct = v * 4 + (2 * n + k)
                        c = c_all[:, bass.ds(ct, 1), :].rearrange("p a n -> p (a n)")
                        V.tensor_tensor(ly[:, :], c, lnr[:, :], ALU.mult).then_inc(ly_ready, 1)
                        att_tile(v + NA // 4, n, k)
                        dve.wait_ge(lt_ready, ct + 1)
                        own.by(V.scalar_tensor_tensor(ly[:, :], lt[:, :], 1.0, ly[:, :], ALU.add, ALU.mult))
                        settle()
                        chi = c_hi[:, bass.ds(ct, 1), :].rearrange("p a n -> p (a n)")
                        own.by(V.tensor_scalar(chi, ly[:, :], 0.5, None, ALU.mult))
                        settle()
                        V.scalar_tensor_tensor(c_lo[:, bass.ds(ct, 1), :].rearrange("p a n -> p (a n)"), ly[:, :], 0.5,
                                               chi.bitcast(F32), ALU.mult, ALU.subtract).then_inc(cn_ready, 1)
                        dve.wait_ge(cn_ready, ct + 1)
            own.endloop(NA // 4)
            with dve.Fori(0, NC_ // 2) as v:
                own.loop(v, 8)
                for n in range(2):
                    for k in range(2):
                        ct = v * 4 + (2 * n + k)
                        dve.wait_ge(tile_done, ct + (KD + 1))
                        dve.wait_ge(gt_loaded[k], v * 32 + (16 * n + 16 + 16 * KD // 2))
                        V.scalar_tensor_tensor(two(ctmp[:, :]), two(gt[:, k, :]), 1.0, PV[k], ALU.add, ALU.mult)\
                            .then_inc(m_taken, 1)
                        dve.wait_ge(m_taken, ct + (KD + 3))
                        own.by(V.tensor_tensor(ly[:, :], ctmp[:, :], m1[:, bass.ds(ct, 1), :].rearrange("p a n -> p (a n)"),
                                               ALU.add))
                        settle()
                        mhi = m_hi[:, bass.ds(ct, 1), :].rearrange("p a n -> p (a n)")
                        own.by(V.tensor_copy(mhi, ly[:, :]))
                        settle()
                        V.tensor_tensor(m_lo[:, bass.ds(ct, 1), :].rearrange("p a n -> p (a n)"), ly[:, :], mhi.bitcast(F32),
                                        ALU.subtract).then_inc(merged_ready, 1)
                        dve.wait_ge(merged_ready, ct + 1)
            own.endloop(NC_ // 2)

            own.by(V.memset(osum[:, :], 0.0))
            settle()
            with dve.Fori(0, NO // 2) as v:
                own.loop(v, 6)
                for n in range(2):
                    ct = v * 2 + n
                    dve.wait_ge(unit_done, ct + (NZ + 1))
                    dve.wait_ge(xt_loaded[n], v * 16 + 16)
                    dve.wait_ge(x2_stored[n], v * 16 + 1)
                    V.scalar_tensor_tensor(two(x2[:, n, :]), PV[n], 0.5, two(xt[:, n, :]), ALU.mult, ALU.add)\
                        .then_inc(x2_ready, 1)
                    dve.wait_ge(x2_ready, ct + 3)
                    hhi = h2_hi[:, bass.ds(ct, 1), :].rearrange("p a n -> p (a n)")
                    g2 = par[:, bass.ds(ct + P_G2, 1)]
                    own.by(V.tensor_scalar(hhi, x2[:, n, :], g2, None, ALU.mult))
                    own.by(V.tensor_tensor(osq[:, :], x2[:, n, :], x2[:, n, :], ALU.mult))
                    settle()
                    V.scalar_tensor_tensor(h2_lo[:, bass.ds(ct, 1), :].rearrange("p a n -> p (a n)"), x2[:, n, :], g2,
                                           hhi.bitcast(F32), ALU.mult, ALU.subtract).then_inc(h2_ready, 1)
                    own.by(V.tensor_tensor(osum[:, :], osum[:, :], osq[:, :], ALU.add))
                    settle()
            own.endloop(NO // 2)
            V.tensor_copy(osq[:, :], osum[:, :]).then_inc(osum_ready, 1)
            dve.wait_ge(ostd_ready, 1)
            V.reciprocal(rs2[:, :], rs2[:, :]).then_inc(rs2_ready, 1)
            dve.wait_ge(rs2_ready, 1)
            with dve.Fori(0, NQ // 2) as v:
                for n in range(2):
                    dve.wait_ge(unit_done, v * 2 + (n + 1 + NZ + NO))
                    V.tensor_tensor(two(qp[:, bass.ds(v * 2 + n, 1), :].rearrange("p a n -> p (a n)")), PV[n], two(rs2[:, :]),
                                    ALU.mult).then_inc(qp_ready, 1)

            iota = late_sb[:, L_IOTA:L_IOTA + NKEY]
            iota16 = late_sb[:, L_IOTA16:L_IOTA16 + 16]
            lists = [(s, h) for s in range(2) for h in range(NH)]
            wkv = wk[:, :].rearrange("p (s h n) -> p s h n", s=2, h=NH)
            cwk = sc[:, :, :, :].rearrange("p s h n -> p (s h n)").rearrange("p (h n) -> p h n", h=NH)
            wk4 = wk[:, :].rearrange("p (x k a) -> p x k a", x=NH, k=TOPK)
            for tt in range(TT):
                dve.wait_ge(scores_ready, tt + 1)
                own.by(V.tensor_copy(sc[:, 0, :, :].rearrange("p h n -> p (h n)"), S[:, :, :].rearrange("p a n -> p (a n)")))
                V.tensor_copy(sc[:, 1, :, :].rearrange("p h n -> p (h n)"), TO[:, :, :].rearrange("p a n -> p (a n)"))\
                    .then_inc(scores_taken, 1)
                dve.wait_ge(scores_taken, tt + 1)
                for s, h in lists:
                    own.by(V.max(tv[:, s, h, 0:8], sc[:, s, h, :]))
                settle()
                for s, h in lists:
                    own.by(V.match_replace(wkv[:, s, h, :], tv[:, s, h, 0:8], sc[:, s, h, :], -3e38))
                settle()
                for s, h in lists:
                    own.by(V.max(tv[:, s, h, 8:16], wkv[:, s, h, :]))
                    own.by(V.max_index(ti[:, s, h, 0:8], tv[:, s, h, 0:8], sc[:, s, h, :]))
                settle()
                for s, h in lists:
                    own.by(V.max_index(ti[:, s, h, 8:16], tv[:, s, h, 8:16], wkv[:, s, h, :]))
                own.by(V.tensor_tensor(cand[:, :, :].rearrange("p h (a b) -> p h a b", a=TOPK),
                                       tv[:, 0, :, :].unsqueeze(3).broadcast_to([P, NH, TOPK, TOPK]),
                                       tv[:, 1, :, :].unsqueeze(2).broadcast_to([P, NH, TOPK, TOPK]), ALU.add))
                settle()
                for h in range(NH):
                    own.by(V.max(sel[:, h, 0:8], cand[:, h, :]))
                settle()
                for h in range(NH):
                    own.by(V.match_replace(cwk[:, h, :], sel[:, h, 0:8], cand[:, h, :], -3e38))
                settle()
                for h in range(NH):
                    own.by(V.max(sel[:, h, 8:16], cwk[:, h, :]))
                    own.by(V.max_index(ju[:, h * TOPK:h * TOPK + 8], sel[:, h, 0:8], cand[:, h, :]))
                settle()
                for h in range(NH):
                    own.by(V.max_index(ju[:, h * TOPK + 8:h * TOPK + 16], sel[:, h, 8:16], cwk[:, h, :]))
                settle()
                own.by(V.tensor_scalar(jab[:, 0, :], ju[:, :], 4, None, ALU.logical_shift_right))
                own.by(V.tensor_scalar(jab[:, 1, :], ju[:, :], 15, None, ALU.bitwise_and))
                own.by(V.tensor_copy(tif[:, :, :], ti[:, :, :, :].rearrange("p s h k -> p s (h k)")))
                if tt:
                    dve.wait_ge(chosen_t, tt)
                own.by(V.tensor_tensor(ssub[:, :].rearrange("p (h k) -> p h k", h=NH), sel[:, :, :],
                                       sel[:, :, 0:1].broadcast_to([P, NH, TOPK]), ALU.subtract))
                settle()
                own.by(V.tensor_copy(jf[:, :, :], jab[:, :, :]))
                settle()
                for s in range(2):
                    own.by(V.tensor_tensor(wk[:, :].rearrange("p (x a) -> p x a", a=TOPK),
                                           jf[:, s, :].unsqueeze(2).broadcast_to([P, NH * TOPK, TOPK]),
                                           iota16.unsqueeze(1).broadcast_to([P, NH * TOPK, TOPK]), ALU.is_equal))
                    settle()
                    own.by(V.tensor_tensor(wk4, wk4,
                                           tif[:, s, :].rearrange("p (h a) -> p h a", h=NH).unsqueeze(2)
                                           .broadcast_to([P, NH, TOPK, TOPK]), ALU.mult))
                    settle()
                    ins = V.tensor_reduce(isel[:, s, :], wk[:, :].rearrange("p (x a) -> p x a", a=TOPK), AX.X, ALU.add)
                    if s == 0:
                        own.by(ins)
                        settle()
                    else:
                        ins.then_inc(chosen, 1)
                        dve.wait_ge(chosen, tt + 1)

            dve.wait_ge(gsum_ready, 1)
            grec = wk[:, 0:T]
            own.by(V.reciprocal(two(grec), TOV))
            settle()
            own.by(V.tensor_tensor(e_t[:, :], e_t[:, :], grec, ALU.mult))
            settle()
            own.by(V.tensor_copy(g_hi[:, :], e_t[:, :]))
            settle()
            own.by(V.tensor_tensor(e_t[:, :], e_t[:, :], g_hi[:, :].bitcast(F32), ALU.subtract))
            settle()
            with dve.Fori(0, NGB // 2) as v:
                for gq in range(8):
                    dve.wait_ge(grp_done, v * 8 + (gq + 1))
                    for q in range(4):
                        t = v * (2 * GB) + (gq * 4 + q)
                        sl = 4 * (gq % 2) + q
                        c1, c2 = i1_t[:, bass.ds(t, 1)], i2_t[:, bass.ds(t, 1)]
                        V.tensor_scalar(oh2[:, sl, :], iota, c2, None, ALU.is_equal)
                        V.tensor_scalar(oh1h[:, sl, :], iota, c1, g_hi[:, bass.ds(t, 1)].bitcast(F32), ALU.is_equal, ALU.mult)
                        ins = V.tensor_scalar(oh1l[:, sl, :], iota, c1, e_t[:, bass.ds(t, 1)], ALU.is_equal, ALU.mult)
                    ins.then_inc(oh_ready, 1)

            def prep(par_, c):
                a = a_st[:, c, :]
                own.by(V.tensor_tensor(a.rearrange("p (b n) -> p b n", n=GB), a.rearrange("p (b n) -> p b n", n=GB),
                                       gl_st[:, :, c, :], ALU.mult))
                settle()
                own.by(V.tensor_copy(wt_hi[:, par_, c, :], a))
                settle()
                V.tensor_tensor(wt_lo[:, par_, c, :], a, wt_hi[:, par_, c, :].bitcast(F32), ALU.subtract).then_inc(w_prepped, 1)

            def add(q, d, k):
                dve.wait_ge(tile_done, q + (2 * KD + 1))
                V.tensor_tensor(two(acc[:, d, :]), PV[k], two(acc[:, d, :]), ALU.add).then_inc(acc_added, 1)

            dve.wait_ge(unit_done, NZ + NO + NQ + NU)
            dve.wait_ge(al_loaded, 16)
            dve.wait_ge(gl_loaded, 16)
            for c in range(GRP):
                prep(0, c)
            dve.wait_ge(acc_loaded, 16)

            def group(g, par_, more):
                for n in range(GRP):
                    for k in range(2):
                        q = g * KD + (2 * n + k)
                        dve.wait_ge(acc_added, q + 1)
                        add(q, 2 * n + k, k)
                    if more and 3 <= n < 7:
                        if n == 3:
                            dve.wait_ge(al_loaded, g * 16 + 32)
                            dve.wait_ge(gl_loaded, g * 16 + 32)
                        prep(1 - par_, 2 * (n - 3))
                        prep(1 - par_, 2 * (n - 3) + 1)

            with dve.Fori(0, NGRP // 2 - 1) as v:
                own.loop(v, 4 * GRP)
                group(v * 2, 0, True)
                group(v * 2 + 1, 1, True)
            own.endloop(NGRP // 2 - 1)
            group(NGRP - 2, 0, True)
            group(NGRP - 1, 1, False)

        @block.tensor
        def _(pe):
            mm = nc.tensor.matmul

            def product(out, slot, w0, ks, rhs_hi, rhs_lo, hooks=None):
                last = None
                n = len(ks)
                for x, k in enumerate(ks):
                    wh = w_hi[:, slot, (w0 + x) * P:(w0 + x + 1) * P]
                    wl = w_lo[:, slot, (w0 + x) * P:(w0 + x + 1) * P]
                    for y, (a, b) in enumerate(((wh, rhs_hi), (wh, rhs_lo), (wl, rhs_hi))):
                        for f in range(2):
                            last = mm(out[:, f, :], a, b[:, k, f * HT:(f + 1) * HT],
                                      start=(x == 0 and y == 0), stop=(x == n - 1 and y == 2))
                    if hooks and x in hooks:
                        hooks[x]()
                return last

            ident = cst[:, C_ID:C_ID + P]
            blk = cst[:, C_BLK:C_BLK + P]
            perm = cst[:, C_PERM:C_PERM + P]
            ones = cst[:, C_ONES:C_ONES + P]
            neg = cst[0:1, C_NEG:C_NEG + CHUNK]

            def spread(out, m, src, start=True, stop=True):
                for f in range(2):
                    last = mm(out[:, f, 0:HT], m, src[:, f * HT:(f + 1) * HT], start=start, stop=stop)
                return last

            pe.sem_inc(grp_done, 2)
            pe.wait_ge(const_loaded, 48)
            pe.wait_ge(xsq_added, KD)
            spread(S, ones, xsum).then_inc(stat_ready, 1)
            pe.wait_ge(xlo_ready, KD)

            def stats(h, i):
                pe.wait_ge(sq_ready, h * 3 + (i + 1))
                pe.wait_ge(std_ready, h * 3 + (i + 2))
                if i == 2:
                    pe.wait_ge(exp_done, h * STEPS + STEPS + 1)
                spread(S, ones if i == 2 else blk, sq).then_inc(stat_ready, 1)

            def rot(h, i):
                pe.wait_ge(z_taken, h * 7 + (i + 1))
                if i == 0:
                    pe.wait_ge(o_ready, h * STEPS + 1)
                else:
                    pe.wait_ge(rot_taken, h * 2 + i)
                spread(TO, perm, xg).then_inc(rot_ready, 1)

            def values(h, j):
                pe.wait_ge(zb_full, h * ZPH + 5)
                pe.wait_ge(rot_taken, h * 2 + 2)
                for b in range(QT):
                    nc.tensor.transpose(TO[:, 0, b * P:(b + 1) * P], zb[:, j, b * P:(b + 1) * P], ident)
                nc.tensor.transpose(TO[0:TS, 1, 0:P], zb[:, j, TP:T], ident).then_inc(vt_ready, 1)

            def carry(out):
                mm(out, ident, ident[:, 0:2], start=True, stop=True)

            def scores(h, i):
                g = h * STEPS + i
                if i == 0:
                    pe.wait_ge(norm_done, h * 3 + 2 + 1)
                    pe.wait_ge(std_ready, h * 3 + 4)
                else:
                    pe.wait_ge(exp_done, g + 1)
                if i == QT:
                    pe.wait_ge(past_loaded, h * 32 + 32)
                    carry(S[:, 0, 510:512])
                for c in range(2):
                    d = slice(c * DH, (c + 1) * DH)
                    if i < QT:
                        mm(S[:, c, 0:(i + 1) * P], q_t[d, i * P:(i + 1) * P], kn_t[d, 0:(i + 1) * P], start=True, stop=False)
                        last = mm(S[:, c, i * P + CHUNK:(i + 1) * P], blk[0:1, :], neg, start=False, stop=True)
                    else:
                        mm(S[0:TS, c, 0:PAST], q_t[d, TP:T], pk[d, :], start=True, stop=True)
                        last = mm(S[0:TS, c, PAST:PAST + TS], q_t[d, TP:T], kn_t[d, TP:T], start=True, stop=True)
                last.then_inc(sc_ready, 1)

            def weights_t(h, i):
                g = h * STEPS + i
                pe.wait_ge(a_ready, g + 1)
                if i == 0:
                    pe.wait_ge(v_ready, h + 1)
                pe.wait_ge(at_ready, g + 1)
                if i == QT:
                    carry(TO[:, 0, 510:512])
                if i < QT:
                    for b in range(i + 1):
                        last = nc.tensor.transpose(TO[:, 0, b * P:(b + 1) * P], e[:, 0, b * P:(b + 1) * P], ident)
                else:
                    for b in range(2):
                        nc.tensor.transpose(TO[:, 0, b * TS:(b + 1) * TS], e[0:TS, 0, b * P:(b + 1) * P], ident[0:TS, 0:TS])
                    last = nc.tensor.transpose(TO[0:TS, 0, 2 * TS:3 * TS], e[0:TS, 0, PAST:PAST + TS], ident[0:TS, 0:TS])
                last.then_inc(tr_ready, 1)

            def mix_values(h, i):
                g = h * STEPS + i
                pe.wait_ge(at_ready, g + 1 + 1)
                pe.wait_ge(o_ready, g + 1)
                if i < QT:
                    for b in range(i + 1):
                        last = mm(TO[:, 1, 0:P], v_tok[:, b, :], a_t[:, b * P:(b + 1) * P], start=(b == 0), stop=(b == i))
                else:
                    for b in range(2):
                        mm(TO[:, 1, 0:TS], pv[:, b, :], a_t[:, b * TS:(b + 1) * TS], start=(b == 0), stop=False)
                    last = mm(TO[:, 1, 0:TS], v_smp[0:TS, :], a_t[0:TS, 2 * TS:3 * TS], start=False, stop=True)
                last.then_inc(av_ready, 1)

            def head_hooks(h, r):
                at = {(1, 1): lambda: stats(h, 0), (1, 2): lambda: rot(h, 0),
                      (2, 1): lambda: stats(h, 1), (2, 2): lambda: rot(h, 1),
                      (3, 1): lambda: values(h, r % 2)}
                slots = [(i, q) for i in range(3, ZPH) for q in range(4)]
                for s in range(STEPS):
                    for d, f in ((0, scores), (3, weights_t), (4, mix_values)):
                        key = slots[4 * s + d]
                        old = at.get(key)
                        at[key] = (lambda f=f, s=s, old=old: ((old() if old else None), f(h, s)))
                at[slots[22]] = lambda: stats(h, 2)
                return at

            def order(hooks, i):
                return {4 * q + 3: hooks[(i, q)] for q in range(4) if (i, q) in hooks}

            with pe.Fori(0, NH // 2) as hp:
                for r in range(2):
                    hooks = head_hooks(hp * 2 + r, r)
                    for i in range(ZPH):
                        n = r * ZPH + i
                        un = hp * (2 * ZPH) + n
                        pe.wait_ge(lo_ready, un + 1)
                        pe.wait_ge(zb_full, un + 1)
                        product(PV[n % 2], n % 2, 0, range(KD), h_hi, h_lo, order(hooks, i)).then_inc(unit_done, 1)

            pe.wait_ge(zb_full, NZ + 2)
            pe.wait_ge(std_ready, 3 * NH + 2)
            pe.wait_ge(conv_done, NH + 1)
            for k in range(KC):
                last = spread(S, ones, c_all[:, k, :], start=(k == 0), stop=(k == KC - 1))
            last.then_inc(mean_ready, 1)
            pe.wait_ge(norm_done, 3 * NH + 1)

            def merge_unit(v, n, unit0, rhs_hi, rhs_lo):
                pe.wait_ge(lo_ready, v * 2 + (n + 1 + NZ + unit0))
                for k in range(2):
                    pe.wait_ge(m_taken, v * 4 + (2 * n + k + 1 + 2 * unit0))
                    product(PV[k], n, KC * k, range(KC), rhs_hi, rhs_lo).then_inc(tile_done, 1)

            with pe.Fori(0, NA // 4) as v:
                for n in range(2):
                    merge_unit(v, n, 0, o_hi, o_lo)
            pe.wait_ge(csq_ready, 1)
            spread(TO, ones, ctmp).then_inc(var_ready, 1)
            with pe.Fori(0, NA // 4) as v:
                for n in range(2):
                    merge_unit(v, n, NA // 2, o_hi, o_lo)
            pe.wait_ge(cn_ready, KC)
            with pe.Fori(0, NC_ // 2) as v:
                for n in range(2):
                    merge_unit(v, n, NA, c_hi, c_lo)

            pe.wait_ge(m_taken, 2 + 2 * KD)
            pe.wait_ge(merged_ready, KD)
            with pe.Fori(0, NO // 2) as v:
                for n in range(2):
                    pe.wait_ge(lo_ready, v * 2 + (n + 1 + U_OUT))
                    pe.wait_ge(x2_ready, v * 2 + (n + 1))
                    product(PV[n], n, 0, range(KD), m_hi, m_lo).then_inc(unit_done, 1)
            pe.wait_ge(x2_ready, 2 + NO)
            pe.wait_ge(h2_ready, KD)

            def rms2():
                pe.wait_ge(osum_ready, 1)
                spread(S, ones, osq).then_inc(ostat_ready, 1)

            for n in range(2):
                pe.wait_ge(lo_ready, n + 1 + U_PQ)
                product(PV[n], n, 0, range(KD), h2_hi, h2_lo, {3: rms2} if n == 0 else None).then_inc(unit_done, 1)
            with pe.Fori(1, NQ // 2) as v:
                for n in range(2):
                    pe.wait_ge(lo_ready, v * 2 + (n + 1 + U_PQ))
                    pe.wait_ge(qp_ready, v * 2 + (n - 1))
                    product(PV[n], n, 0, range(KD), h2_hi, h2_lo).then_inc(unit_done, 1)
            pe.wait_ge(qp_ready, NQ)
            pe.wait_ge(late_loaded, 32)

            def u_unit(v, n, hooks=None):
                pe.wait_ge(lo_ready, v * 2 + (n + 1 + U_PU))
                pe.wait_ge(ab_full, v * 2 + (n + 1))
                product(PV[n], n, 0, range(KD), h2_hi, h2_lo, hooks).then_inc(unit_done, 1)

            for tt in range(TT):
                w = TS if tt == TT - 1 else P
                if tt:
                    pe.wait_ge(chosen_taken, tt)
                for s, bank in ((0, S), (1, TO)):
                    d = slice(s * DH, (s + 1) * DH)
                    for h in range(NH):
                        last = mm(bank[0:w, h // 4, (h % 4) * P:(h % 4 + 1) * P], qp[d, h, tt * P:tt * P + w], ksb[d, :],
                                  start=True, stop=True)
                last.then_inc(scores_ready, 1)
                with pe.Fori(0, TOPK_UNITS // 2) as v:
                    for n in range(2):
                        u_unit(v + tt * TOPK_UNITS // 2, n)
                pe.wait_ge(chosen, tt + 1)
                for x, src in enumerate((ssub[:, :], isel[:, 0, :], isel[:, 1, :])):
                    last = nc.tensor.transpose(S[:, 0, x * P:x * P + w], src[0:w, :], ident[0:w, 0:w])
                last.then_inc(chosen_t, 1)
            pe.wait_ge(chosen_taken, TT)
            spread(TO, late_sb[:, L_BLK16:L_BLK16 + P], e_t).then_inc(gsum_ready, 1)

            banks = [S[:, 0, :], S[:, 1, :], TO[:, 0, :], TO[:, 1, :]]
            v0 = TT * TOPK_UNITS // 2
            with pe.Fori(0, NGB // 2) as v:
                for b in range(2):
                    for n in range(2):
                        def gates(q, b=b, n=n):
                            gq = 4 * b + 2 * n + q
                            pe.wait_ge(oh_ready, v * 8 + (gq + 1))
                            pe.wait_ge(grp_taken, v * 8 + (gq + 1))
                            bank = banks[gq % 4]
                            for t in range(4):
                                sl = 4 * (gq % 2) + t
                                mm(bank[:, t * P:(t + 1) * P], oh2[:, sl, :], oh1h[:, sl, :], start=True, stop=False)
                                last = mm(bank[:, t * P:(t + 1) * P], oh2[:, sl, :], oh1l[:, sl, :], start=False, stop=True)
                            last.then_inc(grp_done, 1)
                        u_unit(v * 2 + (v0 + b), n, {3: lambda g=gates: g(0), 11: lambda g=gates: g(1)})
            v1 = v0 + NGB
            with pe.Fori(0, NU // 2 - v1) as v:
                for n in range(2):
                    u_unit(v + v1, n)

            pe.wait_ge(ab_full, 2 + NU)
            with pe.Fori(0, NGRP // 2) as v:
                for b in range(2):
                    pe.wait_ge(w_prepped, v * (2 * GRP) + (b + 1) * GRP)
                    for n in range(GRP):
                        pe.wait_ge(lo_ready, v * (2 * GRP) + (b * GRP + n + 1 + U_PV))
                        for k in range(2):
                            pe.wait_ge(acc_added, v * (2 * KD) + (b * KD + 2 * n + k + 1))
                            last = None
                            for c in range(GRP):
                                o = (c * 2 + k) * P
                                wh, wl = w_hi[:, n % 2, o:o + P], w_lo[:, n % 2, o:o + P]
                                for y, (a, r_) in enumerate(((wh, wt_hi), (wh, wt_lo), (wl, wt_hi))):
                                    for f in range(2):
                                        last = mm(PV[k][:, f, :], a, r_[:, b, c, f * HT:(f + 1) * HT],
                                                  start=(c == 0 and y == 0), stop=(c == GRP - 1 and y == 2))
                            last.then_inc(tile_done, 1)


def _constants():
    half = DH // 2
    inv = (10000.0 ** (-np.arange(half, dtype=np.float32) / half)).astype(np.float32)
    ang = np.arange(TP, dtype=np.float32)[None, :] * np.tile(inv, P // half)[:, None]
    i = np.arange(P)
    blk = (i[:, None] // DH == i[None, :] // DH).astype(np.float32)
    perm = np.zeros((P, P), np.float32)
    for m in range(P):
        if m % DH < half:
            perm[m + half, m] = -1.0
        else:
            perm[m - half, m] = 1.0
    c = np.zeros((P, C_END), np.float32)
    c[:, C_COS:C_COS + TP] = np.cos(ang)
    c[:, C_SIN:C_SIN + TP] = np.sin(ang)
    c[:, C_ID:C_ID + P] = np.eye(P)
    c[:, C_BLK:C_BLK + P] = blk
    c[:, C_PERM:C_PERM + P] = perm
    c[:, C_ONES:C_ONES + P] = 1.0
    c[:, C_NEG:C_NEG + 64] = -1e30
    late = np.zeros((P, L_END), np.float32)
    late[:, L_IOTA:L_IOTA + P] = i[None, :]
    late[:, L_IOTA16:L_IOTA16 + 16] = np.arange(16)[None, :]
    late[:, L_BLK16:L_BLK16 + P] = i[:, None] // TOPK == i[None, :] // TOPK
    return c, late


def _tiles(w):
    k, n = w.shape
    return w.reshape(k // P, P, n // P, P).transpose(2, 1, 0, 3)


def kernel(**inputs):
    import concourse.bacc as _bacc
    from concourse.bass_utils import run_bass_kernel_spmd as _run

    a = {k: np.asarray(v) for k, v in inputs.items()}
    f = np.float32
    z = _tiles(a["w_in"][0])
    order = []
    for h in range(NH):
        order += [16 + h, 24 + h, 32 + h, h, 8 + h, 40 + 2 * h, 41 + 2 * h, 56 + 2 * h, 57 + 2 * h]
    w_all = np.empty((UNITS, P, UNITW), a["w_in"].dtype)
    w_all[:NZ] = z[order].reshape(NZ, P, UNITW)
    for u0, name in ((U_ATT, "w_attn_out"), (U_ATT + NA, "w_conv_out")):
        t = _tiles(a[name][0]).reshape(NA, 2, P, KC * P).transpose(0, 2, 1, 3)
        w_all[u0:u0 + NA] = t.reshape(NA, P, UNITW)
    w_all[U_OUT:U_PQ] = _tiles(a["w_out"][0]).reshape(NO, P, UNITW)
    w_all[U_PQ:U_PU] = _tiles(a["peer_wq"][0]).reshape(NQ, P, UNITW)
    w_all[U_PU:U_PV] = a["peer_u"][0].reshape(NU, P, KD, P).transpose(0, 3, 2, 1).reshape(NU, P, UNITW)
    w_all[U_PV:] = a["peer_v"][0].reshape(NGRP, GRP, P, 8, DM // 8).transpose(0, 3, 2, 1, 4).reshape(NV, P, UNITW)

    x = np.concatenate([a["x_prompt"][0], a["x_sample"][0]], axis=0)
    x_t = np.ascontiguousarray(x.T.reshape(KD, P, T).transpose(1, 0, 2))
    consts, late = _constants()
    params = np.concatenate([
        a["norm1_g"][0].reshape(KD, P).T, a["norm2_g"][0].reshape(KD, P).T,
        a["conv_dw_w"][0].reshape(TAPS, NH, P).transpose(2, 1, 0).reshape(P, NH * TAPS),
        a["conv_dw_b"][0].reshape(NH, P).T, a["conv_ln_g"][0].reshape(NH, P).T, a["conv_ln_b"][0].reshape(NH, P).T,
        np.tile(a["q_norm_g"][0], 2)[:, None], np.tile(a["k_norm_g"][0], 2)[:, None], a["subln_g"][0][:, None]], axis=1)
    lams = np.broadcast_to(np.stack([a["lambda_q1"][0], a["lambda_q2"][0], a["lambda_k1"][0], a["lambda_k2"][0]])[None],
                           (P, 4, DH))
    keys_t = np.concatenate([a["peer_k1"][0].T, a["peer_k2"][0].T], axis=0)
    past_k = a["cache_attn_k"][0, 0].transpose(1, 2, 3, 0).reshape(NH, P, PAST)
    past_v = a["cache_attn_v"][0, 0].reshape(PAST // P, P, NH, P).transpose(2, 1, 0, 3)
    hist = a["state_conv"][0, 0].T.reshape(NH, P, HIST)
    ins = dict(w_all=w_all, x_t=x_t, consts=consts, late=late, params=params, lams=lams, keys_t=keys_t,
               past_k=past_k, past_v=past_v, hist=hist)
    outs = dict(y_t=(KD, P, T), k_t=(NH, P, T), v_n=(T, NH, P), cst_p=(NH, P, HIST), cst_s=(NH, P, HIST))

    nc = _bacc.Bacc("TRN2", target_bir_lowering=False, num_devices=1)
    arrays = {k: np.ascontiguousarray(v) for k, v in ins.items()}
    aps = {k: nc.dram_tensor(k, v.shape, mybir.dt.from_np(v.dtype), kind="ExternalInput").ap() for k, v in arrays.items()}
    aps |= {k: nc.dram_tensor(k, s, F32, kind="ExternalOutput").ap() for k, s in outs.items()}
    build(nc, **aps)
    r = _run(nc, [arrays], core_ids=[0]).results[0]

    y = r["y_t"].reshape(DM, T).T
    k = r["k_t"].reshape(NH, 2, DH, T).transpose(3, 0, 1, 2)
    v = r["v_n"]

    def state(s):
        return s.reshape(NH * P, HIST).T[None, None]

    return (y[:TP][None], y[TP:][None], k[:TP][None, None], v[:TP][None, None], state(r["cst_p"]),
            k[TP:][None, None], v[TP:][None, None], state(r["cst_s"]))
```

```python
import numpy as np
import concourse.bass as bass
from concourse import mybir
from concourse.alu_op_type import AluOpType as ALU
from contextlib import ExitStack

F32 = mybir.dt.float32
F32R = mybir.dt.float32r
U32 = mybir.dt.uint32
ACT = mybir.ActivationFunctionType
AX = mybir.AxisListType

P = 128
TP, TS = 512, 32
T = TP + TS
HT = T // 2
PAST = 256
DM = 2048
NH = 8
DH = 64
KD = DM // P
KC = 8
TAPS = 31
HIST = TAPS - 1
CHUNK = 64
EPS = 1e-6
LAM0 = 0.8 - 0.6
TOPK = 16
NKEY = 128
UNITW = 2048
NZ, NA, NC_, NO, NQ, NU, NV = 72, 8, 8, 16, 8, 128, 128
U_ATT = NZ
U_OUT = NZ + NA + NC_
U_PQ = U_OUT + NO
U_PU = U_PQ + NQ
U_PV = U_PU + NU
UNITS = U_PV + NV
ZPH = 9
QT = TP // P
STEPS = QT + 1
GRP = 8
NGRP = NKEY // GRP
GB = 16
NGB = T // GB
TOPK_UNITS = 8
TT = 5

C_COS, C_SIN, C_ID, C_BLK, C_PERM, C_ONES, C_NEG, C_END = np.cumsum([0, TP, TP, P, P, P, P, 64]).tolist()
L_IOTA, L_IOTA16, L_BLK16, L_END = np.cumsum([0, P, 16, P]).tolist()
(P_G1, P_G2, P_CW, P_CB, P_LG, P_LB, P_QG, P_KG, P_SUB, P_END) = np.cumsum(
    [0, KD, KD, NH * TAPS, NH, NH, NH, 1, 1, 1]).tolist()
S_EPS, S_NLAM, S_SUB, S_MX, S_NM, S_SUM, S_RC, S_C1, S_L, S_END = 0, 1, 2, 4, 6, 8, 10, 12, 14, 18


class Count:

    def __init__(self, sem):
        self.sem, self.base, self.n = sem, 0, 0

    def by(self, ins, k=1):
        self.n += k
        return ins.then_inc(self.sem, k)

    def value(self):
        return self.base + self.n

    def loop(self, i, per):
        self.outer, self.per = self.base + self.n, per
        self.base, self.n = i * per + self.outer, 0

    def endloop(self, rounds):
        assert self.n == self.per, (self.n, self.per)
        self.base, self.n = self.outer + rounds * self.per, 0


def build(nc, w_all, x_t, consts, late, params, lams, keys_t, past_k, past_v, hist,
          y_t, k_t, v_n, cst_p, cst_s):
    ctx = ExitStack()
    with ctx:
        base = (nc.sbuf_base + 31) // 32 * 32
        top = nc.sbuf_usable_end

        class Area:
            def __init__(self, at, size):
                self.at, self.end = at, at + size

            def take(self, name, shape, dt=F32):
                n = int(np.prod(shape[1:])) * 4
                assert self.at + n <= self.end, (name, self.at + n - self.end)
                t = nc.alloc_sbuf_tensor_at(name, shape, dt, offset=self.at)
                self.at += (n + 31) // 32 * 32
                return t

        BIG = 2 * KD * T * 4
        HALF = BIG // 2
        X0, Y0 = base, base + BIG
        W0 = Y0 + BIG
        M0 = W0 + 6 * UNITW * 4
        wa = Area(W0, 6 * UNITW * 4)
        raw = wa.take("w_raw", [P, 2, UNITW])
        w_hi = wa.take("w_hi", [P, 2, UNITW], F32R)
        w_lo = wa.take("w_lo", [P, 2, UNITW], F32R)
        misc = Area(M0, top - M0)
        cst = misc.take("consts_sb", [P, C_END])
        par = misc.take("params_sb", [P, P_END])
        sm = misc.take("small", [P, S_END])
        MT = misc.at
        MEND = top

        ax = Area(X0, BIG)
        h_hi = ax.take("h_hi", [P, KD, T], F32R)
        h_lo = ax.take("h_lo", [P, KD, T], F32R)
        ay = Area(Y0, BIG)
        o_hi = ay.take("o_hi", [P, KC, T], F32R)
        o_lo = ay.take("o_lo", [P, KC, T], F32R)
        c_all = ay.take("c_all", [P, KC, T])
        zb = ay.take("zb", [P, 2, T])
        xg = ay.take("xg", [P, T])
        sq = ay.take("sq", [P, T])
        rstd = ay.take("rstd", [P, T])
        q_t = ay.take("q_t", [P, T])
        kn_t = ay.take("kn_t", [P, T])
        oraw = ay.take("oraw", [P, T])
        az = Area(MT, MEND - MT)
        v_tok = az.take("v_tok", [P, QT, P])
        v_smp = az.take("v_smp", [P, P])
        pk = az.take("pk", [P, PAST])
        pv = az.take("pv", [P, PAST // P, P])
        e = az.take("e", [P, 2, TP])
        a_t = az.take("a_t", [P, TP])
        u = az.take("u", [P, HIST + TP + HIST + TS])
        rs1 = az.take("rs1", [P, T])
        xs = Area(Y0, HALF).take("xs", [P, KD, T])
        a0 = Area(Y0 + HALF, HALF)
        xsq = a0.take("xsq", [P, KD, T])
        lam_sb = Area(MT, MEND - MT).take("lam_sb", [P, 4, DH])

        am = Area(X0, BIG)
        c_hi = am.take("c_hi", [P, KC, T], F32R)
        c_lo = am.take("c_lo", [P, KC, T], F32R)
        m1 = am.take("m1", [P, KD, T])
        an = Area(Y0, BIG)
        m_hi = an.take("m_hi", [P, KD, T], F32R)
        m_lo = an.take("m_lo", [P, KD, T], F32R)
        ap_ = Area(MT, MEND - MT)
        csq = ap_.take("csq", [P, T])
        ctmp = ap_.take("ctmp", [P, T])
        ly = ap_.take("ly", [P, T])
        lt = ap_.take("lt", [P, T])
        lnr = ap_.take("lnr", [P, T])
        gt = ap_.take("gt", [P, 2, T])
        ao = Area(X0, BIG)
        h2_hi = ao.take("h2_hi", [P, KD, T], F32R)
        h2_lo = ao.take("h2_lo", [P, KD, T], F32R)
        aq = Area(MT, MEND - MT)
        rs2 = aq.take("rs2", [P, T])
        x2 = aq.take("x2", [P, 2, T])
        xt = aq.take("xt", [P, 2, T])
        osq = aq.take("osq", [P, T])
        osum = aq.take("osum", [P, T])
        au = Area(MT, MEND - MT)
        au.take("rs2_again", [P, T])
        ab = au.take("ab", [P, 2, T])
        gb = au.take("gb", [P, 2, T])
        ag = Area(Y0, BIG)
        qp = ag.take("qp", [P, NH, T])
        e_t = ag.take("e_t", [P, T])
        g_hi = ag.take("g_hi", [P, T], F32R)
        i1_t = ag.take("i1_t", [P, T])
        i2_t = ag.take("i2_t", [P, T])
        ksb = ag.take("ksb", [P, NKEY])
        late_sb = ag.take("late_sb", [P, L_END])
        GO = ag.at
        ak = Area(GO, Y0 + BIG - GO)
        sc = ak.take("sc", [P, 2, NH, NKEY])
        wk = ak.take("wk", [P, 2 * NH * NKEY])
        cand = ak.take("cand", [P, NH, TOPK * TOPK])
        tv = ak.take("tv", [P, 2, NH, TOPK])
        ti = ak.take("ti", [P, 2, NH, TOPK], U32)
        tif = ak.take("tif", [P, 2, NH * TOPK])
        sel = ak.take("sel", [P, NH, TOPK])
        ju = ak.take("ju", [P, NH * TOPK], U32)
        jab = ak.take("jab", [P, 2, NH * TOPK], U32)
        jf = ak.take("jf", [P, 2, NH * TOPK])
        ssub = ak.take("ssub", [P, NH * TOPK])
        isel = ak.take("isel", [P, 2, NH * TOPK])
        aw = Area(GO, Y0 + BIG - GO)
        g_st = aw.take("g_st", [P, 2, NKEY, GB])
        oh2 = aw.take("oh2", [P, 8, NKEY], F32R)
        oh1 = aw.take("oh1", [P, 8, 2, NKEY], F32R)
        avx, avy = Area(X0, BIG), Area(Y0, BIG)
        acc = avx.take("acc", [P, KD, T])
        a_st = avy.take("a_st", [P, GRP, T])
        gl_st = avy.take("gl_st", [P, NGB, GRP, GB])
        wt_hi = [a.take(f"wt_hi{i}", [P, GRP, T], F32R) for i, a in enumerate((avy, avx))]
        wt_lo = [a.take(f"wt_lo{i}", [P, GRP, T], F32R) for i, a in enumerate((avy, avx))]

        pair = [ctx.enter_context(nc.psum_tensor(f"pair{i}", [P, 2, 512], F32)) for i in range(2)]
        S = ctx.enter_context(nc.psum_tensor("S", [P, 2, 512], F32))
        TO = ctx.enter_context(nc.psum_tensor("TO", [P, 2, 512], F32))
        PV = [p[:, :, 0:HT] for p in pair]
        SV, TOV = S[:, :, 0:HT], TO[:, :, 0:HT]

        def two(ap):
            return ap.rearrange("p (a b) -> p a b", a=2)

        gate_scr = nc.dram_tensor("gate_scr", (2 * KD, P, T), F32, kind="Internal").ap()
        x2_scr = nc.dram_tensor("x2_scr", (KD, P, T), F32, kind="Internal").ap()
        a_scr = nc.dram_tensor("a_scr", (NKEY, P, T), F32, kind="Internal").ap()
        g_scr = nc.dram_tensor("g_scr", (NGB, P, NKEY, GB), F32, kind="Internal").ap()

        def sem(name):
            return ctx.enter_context(nc.semaphore(name))

        w_loaded = [sem("w_loaded0"), sem("w_loaded1")]
        hi_ready, lo_ready = sem("hi_ready"), sem("lo_ready")
        unit_done = sem("unit_done")
        tile_done = sem("tile_done")
        dve_step, act_step = sem("dve_step"), sem("act_step")
        const_loaded, late_loaded = sem("const_loaded"), sem("late_loaded")
        x_loaded = [sem(f"x_loaded{i}") for i in range(4)]
        xsq_act, xsq_pool, xsq_dve = sem("xsq_act"), sem("xsq_pool"), sem("xsq_dve")
        xhi_ready, xlo_ready, lam_ready, u_zeroed = sem("xhi_ready"), sem("xlo_ready"), sem("lam_ready"), sem("u_zeroed")
        zb_full, z_taken = sem("zb_full"), sem("z_taken")
        sq_ready, stat_ready, std_ready = sem("sq_ready"), sem("stat_ready"), sem("std_ready")
        rot_ready, rot_taken, norm_done = sem("rot_ready"), sem("rot_taken"), sem("norm_done")
        vt_ready, v_ready = sem("vt_ready"), sem("v_ready")
        k_stored, v_stored, gate_stored = sem("k_stored"), sem("v_stored"), [sem("gate_stored0"), sem("gate_stored1")]
        past_loaded, hist_loaded, glu_ready, conv_done, cstate_stored = (
            sem("past_loaded"), sem("hist_loaded"), sem("glu_ready"), sem("conv_done"), sem("cstate_stored"))
        sc_ready, nmax_ready, exp_done, a_ready = sem("sc_ready"), sem("nmax_ready"), sem("exp_done"), sem("a_ready")
        tr_ready, at_ready, av_ready, o_ready = sem("tr_ready"), sem("at_ready"), sem("av_ready"), sem("o_ready")
        mean_ready, csq_ready, var_ready, lnstd_ready = (
            sem("mean_ready"), sem("csq_ready"), sem("var_ready"), sem("lnstd_ready"))
        ly_ready, lt_ready, cn_ready = sem("ly_ready"), sem("lt_ready"), sem("cn_ready")
        gt_loaded = [sem("gt_loaded0"), sem("gt_loaded1")]
        m_taken, merged_ready = sem("m_taken"), sem("merged_ready")
        xt_loaded = [sem("xt_loaded0"), sem("xt_loaded1")]
        x2_ready, x2_stored, h2_ready = sem("x2_ready"), [sem("x2_stored0"), sem("x2_stored1")], sem("h2_ready")
        osum_ready, ostat_ready, ostd_ready, rs2_ready, qp_ready = (
            sem("osum_ready"), sem("ostat_ready"), sem("ostd_ready"), sem("rs2_ready"), sem("qp_ready"))
        ab_full, ab_scaled, gelu_done = sem("ab_full"), sem("ab_scaled"), sem("gelu_done")
        a_stored = [sem("a_stored0"), sem("a_stored1")]
        scores_ready, scores_taken, chosen, chosen_t, chosen_taken = (
            sem("scores_ready"), sem("scores_taken"), sem("chosen"), sem("chosen_t"), sem("chosen_taken"))
        gsum_ready = sem("gsum_ready")
        oh_ready, grp_done, grp_taken = sem("oh_ready"), sem("grp_done"), sem("grp_taken")
        g_stored = [sem("g_stored0"), sem("g_stored1")]
        acc_loaded = [sem(f"acc_loaded{i}") for i in range(4)]
        al_loaded, gl_loaded, w_prepped = sem("al_loaded"), sem("gl_loaded"), sem("w_prepped")
        acc_added, y_stored = sem("acc_added"), sem("y_stored")

        block = ctx.enter_context(nc.Block())

        @block.sync
        def _(sp):
            def load_w(pairno, slot):
                sp.dma_start(raw[:, slot, :], w_all[bass.ds(pairno * 2 + slot, 1)].rearrange("a p n -> p (a n)"))\
                    .then_inc(w_loaded[slot], 16)

            for s in (av_ready, conv_done, cstate_stored, norm_done, v_stored, tr_ready, exp_done, k_stored, sc_ready,
                      o_ready, at_ready, *gate_stored, *a_stored, *g_stored, *x2_stored):
                sp.sem_inc(s, 1)
            for i in range(4):
                sp.dma_start(xs[:, 4 * i:4 * i + 4, :], x_t[:, 4 * i:4 * i + 4, :]).then_inc(x_loaded[i], 16)
                if i == 1:
                    load_w(0, 0)
            load_w(0, 1)

            def z_loads(hp):
                for r in range(2):
                    h = hp * 2 + r
                    for i in range(ZPH):
                        n = r * ZPH + i
                        sp.wait_ge(lo_ready, hp * (2 * ZPH) + (n + 1))
                        load_w(hp * ZPH + (n // 2 + 1), n % 2)
                        if i == 1:
                            sp.wait_ge(av_ready, h * STEPS + 1)
                            sp.dma_start(pk[:, :], past_k[bass.ds(h, 1)].rearrange("a p n -> p (a n)"))\
                                .then_inc(past_loaded, 16)
                            sp.wait_ge(cstate_stored, h * 32 + 1)
                            sp.dma_start(pv[:, :, :], past_v[bass.ds(h, 1)].rearrange("a p b n -> p (a b) n"))\
                                .then_inc(past_loaded, 16)
                        if i == 2:
                            sp.wait_ge(conv_done, h + 1)
                            sp.dma_start(u[:, HIST + TP:HIST + TP + HIST],
                                         hist[bass.ds(h, 1)].rearrange("a p n -> p (a n)")).then_inc(hist_loaded, 16)
                        if i == 5:
                            sp.wait_ge(norm_done, h * 3 + 3)
                            sp.dma_start(k_t[bass.ds(h, 1)].rearrange("a p n -> p (a n)"), kn_t[:, :])\
                                .then_inc(k_stored, 16)
                            sp.wait_ge(v_ready, h + 1)
                            sp.dma_start(v_n[0:TP, bass.ds(h, 1), :].rearrange("(b p) a n -> p b (a n)", p=P), v_tok[:, :, :])\
                                .then_inc(v_stored, 16)
                            sp.dma_start(v_n[TP:T, bass.ds(h, 1), :].rearrange("p a n -> p (a n)"), v_smp[0:TS, :])\
                                .then_inc(v_stored, 16)
                        if i == 7:
                            sp.wait_ge(glu_ready, h + 1)
                            sp.dma_start(cst_p[bass.ds(h, 1)].rearrange("a p n -> p (a n)"), u[:, TP:TP + HIST])\
                                .then_inc(cstate_stored, 16)
                            o = HIST + TP + TS
                            sp.dma_start(cst_s[bass.ds(h, 1)].rearrange("a p n -> p (a n)"), u[:, o:o + HIST])\
                                .then_inc(cstate_stored, 16)

            with sp.Fori(0, NH // 2) as hp:
                z_loads(hp)

            sp.wait_ge(gate_stored[0], 16 * 2 * NH + 1)
            sp.wait_ge(gate_stored[1], 16 * 2 * NH + 1)
            sp.wait_ge(av_ready, NH * STEPS + 1)
            sp.wait_ge(conv_done, NH + 1)
            sp.wait_ge(cstate_stored, 32 * NH + 1)
            sp.wait_ge(v_stored, 32 * NH + 1)

            def merge_loads(v, gate0, tile0):
                for n in range(2):
                    sp.wait_ge(lo_ready, v * 2 + (n + 1 + NZ + tile0 // 2))
                    load_w(v + ((NZ + tile0 // 2) // 2 + 1), n)
                    for k in range(2):
                        ct = v * 4 + (2 * n + k)
                        sp.wait_ge(m_taken, ct + (tile0 + 1))
                        sp.dma_start(gt[:, k, :], gate_scr[bass.ds(ct + gate0, 1)].rearrange("a p n -> p (a n)"))\
                            .then_inc(gt_loaded[k], 16)

            with sp.Fori(0, NA // 2) as v:
                merge_loads(v, KD, 0)
            with sp.Fori(0, NC_ // 2) as v:
                merge_loads(v, 0, KD)

            sp.wait_ge(m_taken, 2 + 2 * KD)
            with sp.Fori(0, NO // 2) as v:
                for n in range(2):
                    sp.wait_ge(lo_ready, v * 2 + (n + 1 + U_OUT))
                    load_w(v + (U_OUT // 2 + 1), n)
                    sp.wait_ge(x2_ready, v * 2 + (n + 1))
                    sp.dma_start(xt[:, n, :], x_t[:, bass.ds(v * 2 + n, 1), :].rearrange("p a n -> p (a n)"))\
                        .then_inc(xt_loaded[n], 16)
            sp.wait_ge(unit_done, NZ + NO)
            sp.dma_start(ksb[:, :], keys_t).then_inc(late_loaded, 16)
            sp.dma_start(late_sb[:, :], late).then_inc(late_loaded, 16)
            def pq_pu_loads(lo_, hi_):
                with sp.Fori(lo_, hi_) as v:
                    for n in range(2):
                        sp.wait_ge(lo_ready, v * 2 + (n + 1 + U_PQ))
                        load_w(v + (U_PQ // 2 + 1), n)

            g_end = (NQ + TT * TOPK_UNITS + 2 * NGB) // 2 + 2
            pq_pu_loads(0, g_end)
            for s in g_stored:
                sp.wait_ge(s, 16 * NGB // 2 + 1)
            for s in a_stored:
                sp.wait_ge(s, 16 * GRP // 2 + 1)
            sp.wait_ge(oh_ready, NGB * 4)
            sp.wait_ge(grp_done, NGB * 4)

            def load_ag(g):
                sp.dma_start(a_st[:, :, :], a_scr[bass.ds(g * GRP, GRP)].rearrange("c p n -> p c n")).then_inc(al_loaded, 16)
                sp.dma_start(gl_st[:, :, :, :].rearrange("p b c n -> p b (c n)"),
                             g_scr[:, :, bass.ds(g * GRP, GRP), :].rearrange("b p c n -> p b (c n)"))\
                    .then_inc(gl_loaded, 16)

            load_ag(0)
            pq_pu_loads(g_end, (NQ + NU) // 2)
            for s in x2_stored:
                sp.wait_ge(s, 16 * KD // 2 + 1)
            sp.wait_ge(w_prepped, GRP)
            for s in a_stored:
                sp.wait_ge(s, 16 * GRP + 1)
            load_ag(1)
            for n in range(GRP):
                sp.wait_ge(lo_ready, n + 1 + U_PV)
                load_w(U_PV // 2 + 1 + n // 2, n % 2)
                if n == 0:
                    sp.wait_ge(unit_done, NZ + NO + NQ + NU)
                if n < 2:
                    for i in (2 * n, 2 * n + 1):
                        sp.dma_start(acc[:, 4 * i:4 * i + 4, :], x2_scr[4 * i:4 * i + 4].rearrange("c p n -> p c n"))\
                            .then_inc(acc_loaded[i], 16)
            for s in a_stored:
                sp.wait_ge(s, 16 * NU // 2 + 1)
            sp.wait_ge(w_prepped, 2 * GRP)
            load_ag(2)
            with sp.Fori(1, NGRP - 2) as g:
                for n in range(GRP):
                    sp.wait_ge(lo_ready, g * GRP + (n + 1 + U_PV))
                    load_w(g * (GRP // 2) + (U_PV // 2 + 1 + n // 2), n % 2)
                sp.wait_ge(w_prepped, g * GRP + 2 * GRP)
                load_ag(g + 2)
            for n in range(2 * GRP - 2):
                sp.wait_ge(lo_ready, (NGRP - 2) * GRP + n + 1 + U_PV)
                load_w((NGRP - 2) * (GRP // 2) + U_PV // 2 + 1 + n // 2, n % 2)
            for d in range(KD):
                sp.wait_ge(acc_added, 2 + (NGRP - 1) * KD + d + 1)
                sp.dma_start(y_t[d], acc[:, d, :]).then_inc(y_stored, 16)
            sp.wait_ge(y_stored, 16 * KD)
            sp.wait_ge(k_stored, 16 * NH + 1)

        @block.gpsimd
        def _(pool):
            pool.memset(u[:, 0:HIST], 0.0).then_inc(u_zeroed, 1)

            def lo(w, slot):
                pool.wait_ge(hi_ready, w + 1)
                pool.tensor_tensor(w_lo[:, slot, :], raw[:, slot, :], w_hi[:, slot, :].bitcast(F32), ALU.subtract)\
                    .then_inc(lo_ready, 1)

            for k in range(1, KD, 2):
                pool.wait_ge(x_loaded[k // 4], 16)
                pool.tensor_tensor(xsq[:, k, :], xs[:, k, :], xs[:, k, :], ALU.mult).then_inc(xsq_pool, 1)
                if k == KD // 2 - 1:
                    lo(0, 0)
            lo(1, 1)
            with pool.Fori(1, U_PU // 2 + 1) as v:
                for n in range(2):
                    lo(v * 2 + n, n)
            pool.wait_ge(rs2_ready, 1)
            with pool.Fori(0, NU // 2) as v:
                for n in range(2):
                    pool.wait_ge(ab_full, v * 2 + (n + 1 + 2))
                    pool.tensor_tensor(ab[:, n, :], ab[:, n, :], rs2[:, :], ALU.mult).then_inc(ab_scaled, 1)
                    lo(v * 2 + (n + U_PU + 2), n)
            with pool.Fori(0, NV // 2 - 1) as v:
                for n in range(2):
                    lo(v * 2 + (n + U_PV + 2), n)

        @block.scalar
        def _(act):
            own = Count(act_step)
            for dst, src in ((cst, consts), (par, params)):
                act.dma_start(dst[:, :], src).then_inc(const_loaded, 16)
            act.dma_start(lam_sb[:, :, :], lams).then_inc(const_loaded, 16)
            act.sem_inc(ab_full, 2)

            def hi(pairno, slot):
                act.wait_ge(w_loaded[slot], pairno * 16 + 16)
                act.activation(w_hi[:, slot, :], raw[:, slot, :], ACT.Copy).then_inc(hi_ready, 1)

            act.wait_ge(const_loaded, 48)
            for k in range(KD):
                act.wait_ge(x_loaded[k // 4], 16)
                act.activation(h_hi[:, k, :], xs[:, k, :], ACT.Copy, scale=par[:, P_G1 + k:P_G1 + k + 1])\
                    .then_inc(xhi_ready, 1)
                if k % 4 == 0:
                    act.activation(xsq[:, k, :], xs[:, k, :], ACT.Square).then_inc(xsq_act, 1)
                if k == KD // 2 - 1:
                    hi(0, 0)
            hi(0, 1)
            act.wait_ge(stat_ready, 1)
            act.activation(rs1[:, :], SV, ACT.Sqrt, scale=1.0 / DM, bias=sm[:, S_EPS:S_EPS + 1]).then_inc(std_ready, 1)
            act.wait_ge(lam_ready, 1)
            act.activation(sm[:, S_L + 2:S_L + 4], sm[:, S_L:S_L + 2], ACT.Exp).then_inc(std_ready, 1)

            def std(inv_n):
                act.activation(rstd[:, :], SV, ACT.Sqrt, scale=inv_n, bias=sm[:, S_EPS:S_EPS + 1]).then_inc(std_ready, 1)

            def z_slot(hp, r, i):
                h = hp * 2 + r
                n = r * ZPH + i
                j = n % 2
                un = hp * (2 * ZPH) + n

                def next_hi():
                    act.wait_ge(unit_done, un + 1)
                    hi(hp * ZPH + (n // 2 + 1), j)

                if i >= 5:
                    next_hi()
                act.wait_ge(zb_full, un + 3)
                if i in (0, 1):
                    m = h * 3 + i
                    act.wait_ge(norm_done, m + 1)
                    act.wait_ge(conv_done, h + 1)
                    act.activation(sq[:, :], zb[:, j, :], ACT.Square).then_inc(sq_ready, 1)
                    act.activation(xg[:, :], zb[:, j, :], ACT.Copy, scale=par[:, P_QG + i:P_QG + i + 1]).then_inc(z_taken, 1)
                if i >= 4:
                    act.activation(zb[:, j, :], zb[:, j, :], ACT.Tanh, scale=0.5).then_inc(z_taken, 1)
                if i >= 5:
                    act.wait_ge(z_taken, h * 7 + (i - 1))
                    act.dma_start(gate_scr[bass.ds(h * 2 + ((i - 5) if i < 7 else (KD + i - 7)), 1)].rearrange("a p n -> p (a n)"),
                                  zb[:, j, :]).then_inc(gate_stored[(i - 5) % 2], 16)
                if i < 5:
                    next_hi()
                if i in (0, 1):
                    act.wait_ge(stat_ready, h * 3 + (i + 2))
                    std(1.0 / DH)

            def values_out(h):
                act.wait_ge(vt_ready, h + 1)
                act.wait_ge(v_stored, h * 32 + 1)
                own.by(act.activation(v_tok[:, :, :].rearrange("p b n -> p (b n)"), TO[:, 0, :], ACT.Copy))
                act.activation(v_smp[0:TS, :], TO[0:TS, 1, 0:P], ACT.Copy).then_inc(v_ready, 1)

            def att_exp(g, i):
                pr = TS if i == QT else P
                keys = PAST + TS if i == QT else (i + 1) * P
                act.wait_ge(nmax_ready, g + 1)
                act.wait_ge(tr_ready, g + 1)
                for c in range(2):
                    ins = act.activation(e[0:pr, c, 0:keys], S[0:pr, c, 0:keys], ACT.Exp, scale=DH ** -0.5,
                                         bias=sm[0:pr, S_NM + c:S_NM + c + 1], accum_out=sm[0:pr, S_SUM + c:S_SUM + c + 1])
                    (own.by(ins) if c == 0 else ins.then_inc(exp_done, 1))

            def att_at(g, i):
                act.wait_ge(tr_ready, g + 2)
                act.wait_ge(av_ready, g + 1)
                if i < QT:
                    act.activation(a_t[:, 0:(i + 1) * P], TO[:, 0, 0:(i + 1) * P], ACT.Copy).then_inc(at_ready, 1)
                else:
                    own.by(act.activation(a_t[:, 0:2 * TS], TO[:, 0, 0:2 * TS], ACT.Copy))
                    act.activation(a_t[0:TS, 2 * TS:3 * TS], TO[0:TS, 0, 2 * TS:3 * TS], ACT.Copy).then_inc(at_ready, 1)

            def att_o(h, g, i):
                w = TS if i == QT else P
                act.wait_ge(av_ready, g + 2)
                if i == 0:
                    act.wait_ge(norm_done, h * 3 + 1)
                act.activation(oraw[:, i * P:i * P + w], TO[:, 1, 0:w], ACT.Copy).then_inc(o_ready, 1)
                if i == QT:
                    act.wait_ge(o_ready, g + 2)
                    act.wait_ge(norm_done, h * 3 + 3)
                    act.activation(sq[:, :], oraw[:, :], ACT.Square).then_inc(sq_ready, 1)

            per = 2 * (1 + STEPS + 1)
            with act.Fori(0, NH // 2) as hp:
                own.loop(hp, per)
                for r in range(2):
                    h = hp * 2 + r
                    for i in range(ZPH):
                        s = i - 3
                        g = h * STEPS + s
                        if s > 0:
                            att_o(h, g - 1, s - 1)
                        if 0 <= s < STEPS:
                            att_exp(g, s)
                            if s == 0:
                                values_out(h)
                            att_at(g, s)
                        if s == STEPS:
                            act.wait_ge(stat_ready, h * 3 + 4)
                            std(1.0 / P)
                        z_slot(hp, r, i)
            own.endloop(NH // 2)

            act.wait_ge(unit_done, NZ)

            def merge_hi(v, n, unit0):
                act.wait_ge(tile_done, v * 4 + (2 * n + 2 + 2 * unit0))
                hi(v + ((NZ + unit0) // 2 + 1), n)

            with act.Fori(0, NA // 4) as v:
                for n in range(2):
                    merge_hi(v, n, 0)
            act.wait_ge(var_ready, 1)
            act.activation(lnr[:, :], TOV, ACT.Sqrt, scale=1.0 / (KC * P), bias=sm[:, S_EPS:S_EPS + 1]).then_inc(lnstd_ready, 1)
            with act.Fori(0, NA // 4) as v:
                own.loop(v, 4)
                for n in range(2):
                    for k in range(2):
                        ct = v * 4 + (2 * n + k)
                        act.wait_ge(ly_ready, ct + 1)
                        own.by(act.activation(ly[:, :], ly[:, :], ACT.Identity, scale=par[:, bass.ds(ct + P_LG, 1)],
                                              bias=par[:, bass.ds(ct + P_LB, 1)]))
                        act.wait_ge(act_step, own.value())
                        act.activation(lt[:, :], ly[:, :], ACT.Tanh, scale=0.5).then_inc(lt_ready, 1)
                    merge_hi(v, n, NA // 2)
            own.endloop(NA // 4)
            with act.Fori(0, NC_ // 2) as v:
                for n in range(2):
                    merge_hi(v, n, NA)

            with act.Fori(0, NO // 2) as v:
                for n in range(2):
                    act.wait_ge(x2_ready, v * 2 + (n + 3))
                    act.dma_start(x2_scr[bass.ds(v * 2 + n, 1)].rearrange("a p n -> p (a n)"), x2[:, n, :])\
                        .then_inc(x2_stored[n], 16)
                    act.wait_ge(unit_done, v * 2 + (n + 1 + NZ))
                    hi(v + (U_OUT // 2 + 1), n)
            act.wait_ge(ostat_ready, 1)
            act.activation(rs2[:, :], SV, ACT.Sqrt, scale=1.0 / DM, bias=sm[:, S_EPS:S_EPS + 1]).then_inc(ostd_ready, 1)
            with act.Fori(0, NQ // 2) as v:
                for n in range(2):
                    act.wait_ge(unit_done, v * 2 + (n + 1 + NZ + NO))
                    hi(v + (U_PQ // 2 + 1), n)

            for s in x2_stored:
                act.wait_ge(s, 16 * NO // 2 + 1)

            def u_slot(v, n):
                m = v * 2 + n
                act.wait_ge(unit_done, m + (1 + NZ + NO + NQ))
                act.activation(two(ab[:, n, :]), PV[n], ACT.Copy).then_inc(ab_full, 1)
                hi(v + (U_PU // 2 + 1), n)
                act.wait_ge(ab_scaled, m + 1)
                act.wait_ge(a_stored[n], v * 16 + 1)
                act.activation(gb[:, n, :], ab[:, n, :], ACT.Gelu).then_inc(gelu_done, 1)
                act.wait_ge(gelu_done, m + 1)
                act.dma_start(a_scr[bass.ds(m, 1)].rearrange("a p n -> p (a n)"), gb[:, n, :]).then_inc(a_stored[n], 16)

            for s in range(TT):
                v_end = (s + 1) * TOPK_UNITS // 2 - 1
                with act.Fori(0, TOPK_UNITS // 2 - 1) as v:
                    for n in range(2):
                        u_slot(v + s * TOPK_UNITS // 2, n)
                w = TS if s == TT - 1 else P
                act.wait_ge(chosen_t, s + 1)
                own.by(act.activation(e_t[:, s * P:s * P + w], S[:, 0, 0:w], ACT.Exp))
                own.by(act.activation(i1_t[:, s * P:s * P + w], S[:, 0, P:P + w], ACT.Copy))
                act.activation(i2_t[:, s * P:s * P + w], S[:, 0, 2 * P:2 * P + w], ACT.Copy).then_inc(chosen_taken, 1)
                u_slot(v_end, 0)
                u_slot(v_end, 1)
            v0 = TT * TOPK_UNITS // 2
            with act.Fori(0, NGB // 2) as v:
                for b in range(2):
                    for n in range(2):
                        u_slot(v * 2 + (v0 + b), n)
                    act.wait_ge(grp_taken, v * 8 + (4 * b + 4 + 2))
                    act.dma_start(g_scr[bass.ds(v * 2 + b, 1)].rearrange("a p c t -> p (a c t)"),
                                  g_st[:, b, :, :].rearrange("p c t -> p (c t)")).then_inc(g_stored[b], 16)
            v1 = v0 + NGB
            with act.Fori(0, NU // 2 - v1) as v:
                for n in range(2):
                    u_slot(v + v1, n)
            with act.Fori(0, NV // 2 - 1) as v:
                for n in range(2):
                    act.wait_ge(tile_done, v * 4 + (2 * n + 2 + 4 * NA))
                    hi(v + (U_PV // 2 + 1), n)

        @block.vector
        def _(dve):
            V = nc.vector
            own = Count(dve_step)

            def settle():
                dve.wait_ge(dve_step, own.value())

            for s in (zb_full, m_taken, x2_ready, acc_added, grp_taken):
                dve.sem_inc(s, 2)
            own.by(V.memset(sm[:, :], EPS))
            settle()
            dve.wait_ge(const_loaded, 48)
            for k in range(KD):
                if k % 4 == 2:
                    dve.wait_ge(x_loaded[k // 4], 16)
                    V.tensor_tensor(xsq[:, k, :], xs[:, k, :], xs[:, k, :], ALU.mult).then_inc(xsq_dve, 1)
                dve.wait_ge(xhi_ready, k + 1)
                V.scalar_tensor_tensor(h_lo[:, k, :], xs[:, k, :], par[:, P_G1 + k:P_G1 + k + 1],
                                       h_hi[:, k, :].bitcast(F32), ALU.mult, ALU.subtract).then_inc(xlo_ready, 1)
            own.by(V.tensor_scalar(sm[:, S_SUB:S_SUB + 1], par[:, P_SUB:P_SUB + 1], 1.0 - LAM0, None, ALU.mult))
            own.by(V.tensor_tensor(lam_sb[:, 0:2, :], lam_sb[:, 0:2, :], lam_sb[:, 2:4, :], ALU.mult))
            settle()
            V.tensor_reduce(sm[:, S_L:S_L + 2], lam_sb[:, 0:2, :], AX.X, ALU.add).then_inc(lam_ready, 1)
            dve.wait_ge(std_ready, 2)
            own.by(V.reciprocal(rs1[:, :], rs1[:, :]))
            own.by(V.tensor_tensor(sm[:, S_NLAM:S_NLAM + 1], sm[:, S_L + 3:S_L + 4], sm[:, S_L + 2:S_L + 3], ALU.subtract))
            settle()
            own.by(V.tensor_scalar(sm[:, S_NLAM:S_NLAM + 1], sm[:, S_NLAM:S_NLAM + 1], -LAM0, None, ALU.add))
            settle()

            def evac(hp, r, i):
                h = hp * 2 + r
                j = (r + i) % 2
                dve.wait_ge(unit_done, hp * (2 * ZPH) + (r * ZPH + i + 1))
                if i == 0:
                    dve.wait_ge(gate_stored[0], h * 32 + 1)
                elif i == 1:
                    dve.wait_ge(gate_stored[1], h * 32 + 1)
                elif i in (2, 3):
                    dve.wait_ge(z_taken, h * 7 + (i - 1))
                elif i == 4:
                    dve.wait_ge(vt_ready, h + 1)
                elif i == 5:
                    dve.wait_ge(glu_ready, h + 1)
                elif i == 6:
                    dve.wait_ge(z_taken, h * 7 + 3)
                else:
                    dve.wait_ge(gate_stored[i - 7], h * 32 + 16 + 1)
                if i == 6:
                    dve.wait_ge(glu_ready, h + 1)
                if i == 3:
                    V.scalar_tensor_tensor(two(zb[:, j, :]), PV[j], 0.5, two(rs1[:, :]), ALU.mult, ALU.mult).then_inc(zb_full, 1)
                else:
                    V.tensor_tensor(two(zb[:, j, :]), PV[j], two(rs1[:, :]), ALU.mult).then_inc(zb_full, 1)

            def rope(h, i):
                dve.wait_ge(std_ready, h * 3 + (i + 3))
                own.by(V.reciprocal(rstd[:, :], rstd[:, :]))
                cs = ((slice(0, TP), slice(0, TP)), (slice(TP, T), slice(PAST, PAST + TS)))
                dve.wait_ge(rot_ready, h * 2 + (i + 1))
                for to, fr in cs:
                    own.by(V.tensor_tensor(xg[:, to], xg[:, to], cst[:, fr], ALU.mult))
                s0, t0 = C_SIN, TP - HT
                own.by(V.tensor_tensor(sq[:, 0:HT], TO[:, 0, 0:HT], cst[:, s0:s0 + HT], ALU.mult))
                own.by(V.tensor_tensor(sq[:, HT:TP], TO[:, 1, 0:t0], cst[:, s0 + HT:s0 + TP], ALU.mult))
                V.tensor_tensor(sq[:, TP:T], TO[:, 1, t0:HT], cst[:, s0 + PAST:s0 + PAST + TS], ALU.mult).then_inc(rot_taken, 1)
                dve.wait_ge(rot_taken, h * 2 + (i + 1))
                own.by(V.tensor_tensor(xg[:, :], xg[:, :], sq[:, :], ALU.add))
                settle()
                if i == 0:
                    dve.wait_ge(sc_ready, h * STEPS + 1)
                else:
                    dve.wait_ge(k_stored, h * 16 + 1)
                V.tensor_tensor((kn_t if i else q_t)[:, :], xg[:, :], rstd[:, :], ALU.mult).then_inc(norm_done, 1)

            def att_max(g, i):
                pr = TS if i == QT else P
                keys = PAST + TS if i == QT else (i + 1) * P
                dve.wait_ge(sc_ready, g + 2)
                own.by(V.tensor_reduce(sm[0:pr, S_MX:S_MX + 2], S[0:pr, :, 0:keys], AX.X, ALU.max))
                settle()
                dve.wait_ge(exp_done, g + 1)
                V.tensor_scalar(sm[0:pr, S_NM:S_NM + 2], sm[0:pr, S_MX:S_MX + 2], -(DH ** -0.5), None, ALU.mult)\
                    .then_inc(nmax_ready, 1)

            def att_mix(g, i):
                pr = TS if i == QT else P
                keys = PAST + TS if i == QT else (i + 1) * P
                dve.wait_ge(exp_done, g + 2)
                own.by(V.reciprocal(sm[0:pr, S_RC:S_RC + 2], sm[0:pr, S_SUM:S_SUM + 2]))
                settle()
                own.by(V.tensor_scalar(e[0:pr, 0, 0:keys], e[0:pr, 0, 0:keys], sm[0:pr, S_RC:S_RC + 1], None, ALU.mult))
                own.by(V.tensor_tensor(sm[0:pr, S_C1:S_C1 + 1], sm[0:pr, S_RC + 1:S_RC + 2], sm[0:pr, S_NLAM:S_NLAM + 1], ALU.mult))
                settle()
                V.scalar_tensor_tensor(e[0:pr, 0, 0:keys], e[0:pr, 1, 0:keys], sm[0:pr, S_C1:S_C1 + 1],
                                       e[0:pr, 0, 0:keys], ALU.mult, ALU.add).then_inc(a_ready, 1)

            def glu(h, j):
                dve.wait_ge(z_taken, h * 7 + 3)
                dve.wait_ge(hist_loaded, h * 16 + 16)
                a, b = zb[:, 1 - j, :], zb[:, j, :]
                own.by(V.scalar_tensor_tensor(u[:, HIST:HIST + TP], b[:, 0:TP], 1.0, a[:, 0:TP], ALU.add, ALU.mult))
                V.scalar_tensor_tensor(u[:, HIST + TP + HIST:], b[:, TP:T], 1.0, a[:, TP:T], ALU.add, ALU.mult)\
                    .then_inc(glu_ready, 1)

            def taps(h, lo_, hi_):
                for w in range(lo_, hi_):
                    cw = par[:, bass.ds(h * TAPS + (P_CW + w), 1)]
                    segs = ((0, TP, 0), (TP, T, HIST))
                    if w == 0:
                        dve.wait_ge(glu_ready, h + 1)
                    else:
                        settle()
                    for a, b, sh in segs:
                        src = u[:, a + sh + w:b + sh + w]
                        if w == 0:
                            own.by(V.tensor_scalar(xg[:, a:b], src, cw, par[:, bass.ds(h + P_CB, 1)], ALU.mult, ALU.add))
                        elif w < TAPS - 1:
                            own.by(V.scalar_tensor_tensor(xg[:, a:b], src, cw, xg[:, a:b], ALU.mult, ALU.add))
                        else:
                            dst = c_all[:, bass.ds(h, 1), a:b].rearrange("p a n -> p (a n)")
                            ins = V.scalar_tensor_tensor(dst, src, cw, xg[:, a:b], ALU.mult, ALU.add)
                            (own.by(ins) if a == 0 else ins.then_inc(conv_done, 1))

            def o_norm(h):
                dve.wait_ge(std_ready, h * 3 + 5)
                own.by(V.reciprocal(rstd[:, :], rstd[:, :]))
                settle()
                own.by(V.tensor_tensor(oraw[:, :], oraw[:, :], rstd[:, :], ALU.mult))
                settle()
                sub = sm[:, S_SUB:S_SUB + 1]
                ohi = o_hi[:, bass.ds(h, 1), :].rearrange("p a n -> p (a n)")
                own.by(V.tensor_scalar(ohi, oraw[:, :], sub, None, ALU.mult))
                settle()
                V.scalar_tensor_tensor(o_lo[:, bass.ds(h, 1), :].rearrange("p a n -> p (a n)"), oraw[:, :], sub,
                                       ohi.bitcast(F32), ALU.mult, ALU.subtract).then_inc(norm_done, 1)

            per_head = 2 * 6 + 4 * STEPS + 1 + (2 * TAPS - 1) + 3
            with dve.Fori(0, NH // 2) as hp:
                own.loop(hp, 2 * per_head)
                for r in range(2):
                    h = hp * 2 + r
                    g = h * STEPS
                    evac(hp, r, 0)
                    rope(h, 0)
                    evac(hp, r, 1)
                    rope(h, 1)
                    evac(hp, r, 2)
                    for s in range(2):
                        att_max(g + s, s)
                        att_mix(g + s, s)
                        evac(hp, r, s + 3)
                    glu(h, (r + 4) % 2)
                    taps(h, 0, 2)
                    for s in range(2, STEPS):
                        w = 2 + 8 * (s - 2)
                        att_max(g + s, s)
                        taps(h, w, w + 4)
                        att_mix(g + s, s)
                        taps(h, w + 4, w + 6)
                        evac(hp, r, s + 3)
                        taps(h, w + 6, w + 8)
                    taps(h, 2 + 8 * (STEPS - 2), TAPS)
                    o_norm(h)
                    evac(hp, r, 8)
            own.endloop(NH // 2)

            dve.wait_ge(av_ready, NH * STEPS + 1)
            dve.wait_ge(v_stored, NH * 32 + 1)
            dve.wait_ge(cstate_stored, NH * 32 + 1)
            own.by(V.memset(csq[:, :], 0.0))
            settle()

            def att_tile(v, n, k):
                ct = v * 4 + (2 * n + k)
                dve.wait_ge(tile_done, ct + 1)
                dve.wait_ge(gt_loaded[k], v * 32 + (16 * n + 16))
                V.scalar_tensor_tensor(two(m1[:, bass.ds(ct, 1), :].rearrange("p a n -> p (a n)")), two(gt[:, k, :]), 1.0,
                                       PV[k], ALU.add, ALU.mult).then_inc(m_taken, 1)

            dve.wait_ge(mean_ready, 1)
            with dve.Fori(0, NA // 4) as v:
                own.loop(v, 12)
                for n in range(2):
                    for k in range(2):
                        ct = v * 4 + (2 * n + k)
                        att_tile(v, n, k)
                        c = c_all[:, bass.ds(ct, 1), :].rearrange("p a n -> p (a n)")
                        own.by(V.scalar_tensor_tensor(two(c), SV, -1.0 / (KC * P), two(c), ALU.mult, ALU.add))
                        settle()
                        own.by(V.tensor_tensor(ctmp[:, :], c, c, ALU.mult))
                        settle()
                        own.by(V.tensor_tensor(csq[:, :], csq[:, :], ctmp[:, :], ALU.add))
                        settle()
            own.endloop(NA // 4)
            V.tensor_copy(ctmp[:, :], csq[:, :]).then_inc(csq_ready, 1)
            dve.wait_ge(lnstd_ready, 1)
            own.by(V.reciprocal(lnr[:, :], lnr[:, :]))
            settle()
            with dve.Fori(0, NA // 4) as v:
                own.loop(v, 8)
                for n in range(2):
                    for k in range(2):
                        ct = v * 4 + (2 * n + k)
                        c = c_all[:, bass.ds(ct, 1), :].rearrange("p a n -> p (a n)")
                        V.tensor_tensor(ly[:, :], c, lnr[:, :], ALU.mult).then_inc(ly_ready, 1)
                        att_tile(v + NA // 4, n, k)
                        dve.wait_ge(lt_ready, ct + 1)
                        own.by(V.scalar_tensor_tensor(ly[:, :], lt[:, :], 1.0, ly[:, :], ALU.add, ALU.mult))
                        settle()
                        chi = c_hi[:, bass.ds(ct, 1), :].rearrange("p a n -> p (a n)")
                        own.by(V.tensor_scalar(chi, ly[:, :], 0.5, None, ALU.mult))
                        settle()
                        V.scalar_tensor_tensor(c_lo[:, bass.ds(ct, 1), :].rearrange("p a n -> p (a n)"), ly[:, :], 0.5,
                                               chi.bitcast(F32), ALU.mult, ALU.subtract).then_inc(cn_ready, 1)
                        dve.wait_ge(cn_ready, ct + 1)
            own.endloop(NA // 4)
            with dve.Fori(0, NC_ // 2) as v:
                own.loop(v, 8)
                for n in range(2):
                    for k in range(2):
                        ct = v * 4 + (2 * n + k)
                        dve.wait_ge(tile_done, ct + (KD + 1))
                        dve.wait_ge(gt_loaded[k], v * 32 + (16 * n + 16 + 16 * KD // 2))
                        V.scalar_tensor_tensor(two(ctmp[:, :]), two(gt[:, k, :]), 1.0, PV[k], ALU.add, ALU.mult)\
                            .then_inc(m_taken, 1)
                        dve.wait_ge(m_taken, ct + (KD + 3))
                        own.by(V.tensor_tensor(ly[:, :], ctmp[:, :], m1[:, bass.ds(ct, 1), :].rearrange("p a n -> p (a n)"),
                                               ALU.add))
                        settle()
                        mhi = m_hi[:, bass.ds(ct, 1), :].rearrange("p a n -> p (a n)")
                        own.by(V.tensor_copy(mhi, ly[:, :]))
                        settle()
                        V.tensor_tensor(m_lo[:, bass.ds(ct, 1), :].rearrange("p a n -> p (a n)"), ly[:, :], mhi.bitcast(F32),
                                        ALU.subtract).then_inc(merged_ready, 1)
                        dve.wait_ge(merged_ready, ct + 1)
            own.endloop(NC_ // 2)

            own.by(V.memset(osum[:, :], 0.0))
            settle()
            with dve.Fori(0, NO // 2) as v:
                own.loop(v, 6)
                for n in range(2):
                    ct = v * 2 + n
                    dve.wait_ge(unit_done, ct + (NZ + 1))
                    dve.wait_ge(xt_loaded[n], v * 16 + 16)
                    dve.wait_ge(x2_stored[n], v * 16 + 1)
                    V.scalar_tensor_tensor(two(x2[:, n, :]), PV[n], 0.5, two(xt[:, n, :]), ALU.mult, ALU.add)\
                        .then_inc(x2_ready, 1)
                    dve.wait_ge(x2_ready, ct + 3)
                    hhi = h2_hi[:, bass.ds(ct, 1), :].rearrange("p a n -> p (a n)")
                    g2 = par[:, bass.ds(ct + P_G2, 1)]
                    own.by(V.tensor_scalar(hhi, x2[:, n, :], g2, None, ALU.mult))
                    own.by(V.tensor_tensor(osq[:, :], x2[:, n, :], x2[:, n, :], ALU.mult))
                    settle()
                    V.scalar_tensor_tensor(h2_lo[:, bass.ds(ct, 1), :].rearrange("p a n -> p (a n)"), x2[:, n, :], g2,
                                           hhi.bitcast(F32), ALU.mult, ALU.subtract).then_inc(h2_ready, 1)
                    own.by(V.tensor_tensor(osum[:, :], osum[:, :], osq[:, :], ALU.add))
                    settle()
            own.endloop(NO // 2)
            V.tensor_copy(osq[:, :], osum[:, :]).then_inc(osum_ready, 1)
            dve.wait_ge(ostd_ready, 1)
            V.reciprocal(rs2[:, :], rs2[:, :]).then_inc(rs2_ready, 1)
            dve.wait_ge(rs2_ready, 1)
            with dve.Fori(0, NQ // 2) as v:
                for n in range(2):
                    dve.wait_ge(unit_done, v * 2 + (n + 1 + NZ + NO))
                    V.tensor_tensor(two(qp[:, bass.ds(v * 2 + n, 1), :].rearrange("p a n -> p (a n)")), PV[n], two(rs2[:, :]),
                                    ALU.mult).then_inc(qp_ready, 1)

            iota = late_sb[:, L_IOTA:L_IOTA + NKEY]
            iota16 = late_sb[:, L_IOTA16:L_IOTA16 + 16]
            lists = [(s, h) for s in range(2) for h in range(NH)]
            wkv = wk[:, :].rearrange("p (s h n) -> p s h n", s=2, h=NH)
            cwk = sc[:, :, :, :].rearrange("p s h n -> p (s h n)").rearrange("p (h n) -> p h n", h=NH)
            wk4 = wk[:, :].rearrange("p (x k a) -> p x k a", x=NH, k=TOPK)
            for tt in range(TT):
                dve.wait_ge(scores_ready, tt + 1)
                own.by(V.tensor_copy(sc[:, 0, :, :].rearrange("p h n -> p (h n)"), S[:, :, :].rearrange("p a n -> p (a n)")))
                V.tensor_copy(sc[:, 1, :, :].rearrange("p h n -> p (h n)"), TO[:, :, :].rearrange("p a n -> p (a n)"))\
                    .then_inc(scores_taken, 1)
                dve.wait_ge(scores_taken, tt + 1)
                for s, h in lists:
                    own.by(V.max(tv[:, s, h, 0:8], sc[:, s, h, :]))
                settle()
                for s, h in lists:
                    own.by(V.match_replace(wkv[:, s, h, :], tv[:, s, h, 0:8], sc[:, s, h, :], -3e38))
                settle()
                for s, h in lists:
                    own.by(V.max(tv[:, s, h, 8:16], wkv[:, s, h, :]))
                    own.by(V.max_index(ti[:, s, h, 0:8], tv[:, s, h, 0:8], sc[:, s, h, :]))
                settle()
                for s, h in lists:
                    own.by(V.max_index(ti[:, s, h, 8:16], tv[:, s, h, 8:16], wkv[:, s, h, :]))
                own.by(V.tensor_tensor(cand[:, :, :].rearrange("p h (a b) -> p h a b", a=TOPK),
                                       tv[:, 0, :, :].unsqueeze(3).broadcast_to([P, NH, TOPK, TOPK]),
                                       tv[:, 1, :, :].unsqueeze(2).broadcast_to([P, NH, TOPK, TOPK]), ALU.add))
                settle()
                for h in range(NH):
                    own.by(V.max(sel[:, h, 0:8], cand[:, h, :]))
                settle()
                for h in range(NH):
                    own.by(V.match_replace(cwk[:, h, :], sel[:, h, 0:8], cand[:, h, :], -3e38))
                settle()
                for h in range(NH):
                    own.by(V.max(sel[:, h, 8:16], cwk[:, h, :]))
                    own.by(V.max_index(ju[:, h * TOPK:h * TOPK + 8], sel[:, h, 0:8], cand[:, h, :]))
                settle()
                for h in range(NH):
                    own.by(V.max_index(ju[:, h * TOPK + 8:h * TOPK + 16], sel[:, h, 8:16], cwk[:, h, :]))
                settle()
                own.by(V.tensor_scalar(jab[:, 0, :], ju[:, :], 4, None, ALU.logical_shift_right))
                own.by(V.tensor_scalar(jab[:, 1, :], ju[:, :], 15, None, ALU.bitwise_and))
                own.by(V.tensor_copy(tif[:, :, :], ti[:, :, :, :].rearrange("p s h k -> p s (h k)")))
                if tt:
                    dve.wait_ge(chosen_t, tt)
                own.by(V.tensor_tensor(ssub[:, :].rearrange("p (h k) -> p h k", h=NH), sel[:, :, :],
                                       sel[:, :, 0:1].broadcast_to([P, NH, TOPK]), ALU.subtract))
                settle()
                own.by(V.tensor_copy(jf[:, :, :], jab[:, :, :]))
                settle()
                for s in range(2):
                    own.by(V.tensor_tensor(wk[:, :].rearrange("p (x a) -> p x a", a=TOPK),
                                           jf[:, s, :].unsqueeze(2).broadcast_to([P, NH * TOPK, TOPK]),
                                           iota16.unsqueeze(1).broadcast_to([P, NH * TOPK, TOPK]), ALU.is_equal))
                    settle()
                    own.by(V.tensor_tensor(wk4, wk4,
                                           tif[:, s, :].rearrange("p (h a) -> p h a", h=NH).unsqueeze(2)
                                           .broadcast_to([P, NH, TOPK, TOPK]), ALU.mult))
                    settle()
                    ins = V.tensor_reduce(isel[:, s, :], wk[:, :].rearrange("p (x a) -> p x a", a=TOPK), AX.X, ALU.add)
                    if s == 0:
                        own.by(ins)
                        settle()
                    else:
                        ins.then_inc(chosen, 1)
                        dve.wait_ge(chosen, tt + 1)

            dve.wait_ge(gsum_ready, 1)
            grec = wk[:, 0:T]
            own.by(V.reciprocal(two(grec), TOV))
            settle()
            own.by(V.tensor_tensor(e_t[:, :], e_t[:, :], grec, ALU.mult))
            settle()
            own.by(V.tensor_copy(g_hi[:, :], e_t[:, :]))
            settle()
            own.by(V.tensor_tensor(e_t[:, :], e_t[:, :], g_hi[:, :].bitcast(F32), ALU.subtract))
            settle()
            def one_hot(v, gq):
                for q in range(4):
                    t = v * (2 * GB) + (gq * 4 + q)
                    sl = 4 * (gq % 2) + q
                    c1, c2 = i1_t[:, bass.ds(t, 1)], i2_t[:, bass.ds(t, 1)]
                    V.tensor_scalar(oh2[:, sl, :], iota, c2, None, ALU.is_equal)
                    V.tensor_scalar(oh1[:, sl, 0, :], iota, c1, g_hi[:, bass.ds(t, 1)].bitcast(F32), ALU.is_equal, ALU.mult)
                    ins = V.tensor_scalar(oh1[:, sl, 1, :], iota, c1, e_t[:, bass.ds(t, 1)], ALU.is_equal, ALU.mult)
                ins.then_inc(oh_ready, 1)

            def g_round(v, more):
                for gq in range(8):
                    b = gq // 4
                    dve.wait_ge(grp_done, v * 8 + (gq + 1))
                    if gq % 4 == 0:
                        dve.wait_ge(g_stored[b], v * 16 + 1)
                    part = (S, TO)[gq % 2][:, :, :].rearrange("p a n -> p (a n)").rearrange("p (t h c) -> p t h c", t=4, h=2)
                    t0 = 4 * (gq % 4)
                    dst = g_st[:, b, :, t0:t0 + 4].rearrange("p c t -> p t c")
                    own.by(V.tensor_copy(dst, part[:, :, 0, :]))
                    settle()
                    V.tensor_tensor(dst, dst, part[:, :, 1, :], ALU.add).then_inc(grp_taken, 1)
                    if more or gq < 6:
                        one_hot(v, gq + 2)

            one_hot(0, 0)
            one_hot(0, 1)
            with dve.Fori(0, NGB // 2 - 1) as v:
                own.loop(v, 8)
                g_round(v, True)
            own.endloop(NGB // 2 - 1)
            g_round(NGB // 2 - 1, False)

            def prep(parity, c):
                a = a_st[:, c, :]
                own.by(V.tensor_tensor(a.rearrange("p (b n) -> p b n", n=GB), a.rearrange("p (b n) -> p b n", n=GB),
                                       gl_st[:, :, c, :], ALU.mult))
                settle()
                own.by(V.tensor_copy(wt_hi[parity][:, c, :], a))
                settle()
                V.tensor_tensor(wt_lo[parity][:, c, :], a, wt_hi[parity][:, c, :].bitcast(F32), ALU.subtract).then_inc(w_prepped, 1)

            def add(q, d, k):
                dve.wait_ge(tile_done, q + (2 * KD + 1))
                V.tensor_tensor(two(acc[:, d, :]), PV[k], two(acc[:, d, :]), ALU.add).then_inc(acc_added, 1)

            dve.wait_ge(al_loaded, 16)
            dve.wait_ge(gl_loaded, 16)
            for c in range(GRP):
                prep(0, c)
            dve.wait_ge(unit_done, NZ + NO + NQ + NU)

            def group(g, parity, more):
                for n in range(GRP):
                    for k in range(2):
                        q = g * KD + (2 * n + k)
                        if parity == 0 and k == 0 and n % 2 == 0:
                            dve.wait_ge(acc_loaded[n // 2], 16)
                        dve.wait_ge(acc_added, q + 1)
                        add(q, 2 * n + k, k)
                    if more and 3 <= n < 7:
                        if n == 3:
                            dve.wait_ge(al_loaded, g * 16 + 32)
                            dve.wait_ge(gl_loaded, g * 16 + 32)
                        prep(1 - parity, 2 * (n - 3))
                        prep(1 - parity, 2 * (n - 3) + 1)

            with dve.Fori(0, NGRP // 2 - 1) as v:
                own.loop(v, 4 * GRP)
                group(v * 2, 0, True)
                group(v * 2 + 1, 1, True)
            own.endloop(NGRP // 2 - 1)
            group(NGRP - 2, 0, True)
            group(NGRP - 1, 1, False)

        @block.tensor
        def _(pe):
            mm = nc.tensor.matmul

            def product(out, slot, w0, ks, rhs_hi, rhs_lo, hooks=None):
                last = None
                n = len(ks)
                for x, k in enumerate(ks):
                    wh = w_hi[:, slot, (w0 + x) * P:(w0 + x + 1) * P]
                    wl = w_lo[:, slot, (w0 + x) * P:(w0 + x + 1) * P]
                    for y, (a, b) in enumerate(((wh, rhs_hi), (wh, rhs_lo), (wl, rhs_hi))):
                        for f in range(2):
                            last = mm(out[:, f, :], a, b[:, k, f * HT:(f + 1) * HT],
                                      start=(x == 0 and y == 0), stop=(x == n - 1 and y == 2))
                    if hooks and x in hooks:
                        hooks[x]()
                return last

            ident = cst[:, C_ID:C_ID + P]
            blk = cst[:, C_BLK:C_BLK + P]
            perm = cst[:, C_PERM:C_PERM + P]
            ones = cst[:, C_ONES:C_ONES + P]
            neg = cst[0:1, C_NEG:C_NEG + CHUNK]

            def spread(out, m, src, start=True, stop=True):
                for f in range(2):
                    last = mm(out[:, f, 0:HT], m, src[:, f * HT:(f + 1) * HT], start=start, stop=stop)
                return last

            pe.wait_ge(const_loaded, 48)
            for k in range(KD):
                if k % 2:
                    pe.wait_ge(xsq_pool, k // 2 + 1)
                else:
                    pe.wait_ge(xsq_dve if k % 4 else xsq_act, k // 4 + 1)
                last = spread(S, ones, xsq[:, k, :], start=(k == 0), stop=(k == KD - 1))
            last.then_inc(stat_ready, 1)
            pe.wait_ge(xlo_ready, KD)

            def stats(h, i):
                pe.wait_ge(sq_ready, h * 3 + (i + 1))
                pe.wait_ge(std_ready, h * 3 + (i + 2))
                if i == 2:
                    pe.wait_ge(exp_done, h * STEPS + STEPS + 1)
                spread(S, ones if i == 2 else blk, sq).then_inc(stat_ready, 1)

            def rot(h, i):
                pe.wait_ge(z_taken, h * 7 + (i + 1))
                if i == 0:
                    pe.wait_ge(o_ready, h * STEPS + 1)
                else:
                    pe.wait_ge(rot_taken, h * 2 + i)
                spread(TO, perm, xg).then_inc(rot_ready, 1)

            def values(h, j):
                pe.wait_ge(zb_full, h * ZPH + 5)
                pe.wait_ge(rot_taken, h * 2 + 2)
                for b in range(QT):
                    nc.tensor.transpose(TO[:, 0, b * P:(b + 1) * P], zb[:, j, b * P:(b + 1) * P], ident)
                nc.tensor.transpose(TO[0:TS, 1, 0:P], zb[:, j, TP:T], ident).then_inc(vt_ready, 1)

            def carry(out):
                mm(out, ident, ident[:, 0:2], start=True, stop=True)

            def scores(h, i):
                g = h * STEPS + i
                if i == 0:
                    pe.wait_ge(norm_done, h * 3 + 3)
                    pe.wait_ge(std_ready, h * 3 + 4)
                else:
                    pe.wait_ge(exp_done, g + 1)
                if i == QT:
                    pe.wait_ge(past_loaded, h * 32 + 32)
                    carry(S[:, 0, 510:512])
                for c in range(2):
                    d = slice(c * DH, (c + 1) * DH)
                    if i < QT:
                        mm(S[:, c, 0:(i + 1) * P], q_t[d, i * P:(i + 1) * P], kn_t[d, 0:(i + 1) * P], start=True, stop=False)
                        last = mm(S[:, c, i * P + CHUNK:(i + 1) * P], blk[0:1, :], neg, start=False, stop=True)
                    else:
                        mm(S[0:TS, c, 0:PAST], q_t[d, TP:T], pk[d, :], start=True, stop=True)
                        last = mm(S[0:TS, c, PAST:PAST + TS], q_t[d, TP:T], kn_t[d, TP:T], start=True, stop=True)
                last.then_inc(sc_ready, 1)

            def weights_t(h, i):
                g = h * STEPS + i
                pe.wait_ge(a_ready, g + 1)
                if i == 0:
                    pe.wait_ge(v_ready, h + 1)
                pe.wait_ge(at_ready, g + 1)
                if i == QT:
                    carry(TO[:, 0, 510:512])
                if i < QT:
                    for b in range(i + 1):
                        last = nc.tensor.transpose(TO[:, 0, b * P:(b + 1) * P], e[:, 0, b * P:(b + 1) * P], ident)
                else:
                    for b in range(2):
                        nc.tensor.transpose(TO[:, 0, b * TS:(b + 1) * TS], e[0:TS, 0, b * P:(b + 1) * P], ident[0:TS, 0:TS])
                    last = nc.tensor.transpose(TO[0:TS, 0, 2 * TS:3 * TS], e[0:TS, 0, PAST:PAST + TS], ident[0:TS, 0:TS])
                last.then_inc(tr_ready, 1)

            def mix_values(h, i):
                g = h * STEPS + i
                pe.wait_ge(at_ready, g + 2)
                pe.wait_ge(o_ready, g + 1)
                if i < QT:
                    for b in range(i + 1):
                        last = mm(TO[:, 1, 0:P], v_tok[:, b, :], a_t[:, b * P:(b + 1) * P], start=(b == 0), stop=(b == i))
                else:
                    for b in range(2):
                        mm(TO[:, 1, 0:TS], pv[:, b, :], a_t[:, b * TS:(b + 1) * TS], start=(b == 0), stop=False)
                    last = mm(TO[:, 1, 0:TS], v_smp[0:TS, :], a_t[0:TS, 2 * TS:3 * TS], start=False, stop=True)
                last.then_inc(av_ready, 1)

            def head_hooks(h, r):
                at = {(1, 1): lambda: stats(h, 0), (1, 2): lambda: rot(h, 0),
                      (2, 1): lambda: stats(h, 1), (2, 2): lambda: rot(h, 1),
                      (3, 1): lambda: values(h, r % 2)}
                slots = [(i, q) for i in range(3, ZPH) for q in range(4)]
                for s in range(STEPS):
                    for d, f in ((0, scores), (3, weights_t), (4, mix_values)):
                        key = slots[4 * s + d]
                        old = at.get(key)
                        at[key] = (lambda f=f, s=s, old=old: ((old() if old else None), f(h, s)))
                at[slots[22]] = lambda: stats(h, 2)
                return at

            def order(hooks, i):
                return {4 * q + 3: hooks[(i, q)] for q in range(4) if (i, q) in hooks}

            with pe.Fori(0, NH // 2) as hp:
                for r in range(2):
                    hooks = head_hooks(hp * 2 + r, r)
                    for i in range(ZPH):
                        n = r * ZPH + i
                        un = hp * (2 * ZPH) + n
                        pe.wait_ge(lo_ready, un + 1)
                        pe.wait_ge(zb_full, un + 1)
                        product(PV[n % 2], n % 2, 0, range(KD), h_hi, h_lo, order(hooks, i)).then_inc(unit_done, 1)

            pe.wait_ge(std_ready, 3 * NH + 2)
            pe.wait_ge(conv_done, NH + 1)
            for k in range(KC):
                last = spread(S, ones, c_all[:, k, :], start=(k == 0), stop=(k == KC - 1))
            last.then_inc(mean_ready, 1)
            pe.wait_ge(zb_full, NZ + 2)
            pe.wait_ge(norm_done, 3 * NH + 1)

            def merge_unit(v, n, unit0, rhs_hi, rhs_lo, hooks=None):
                pe.wait_ge(lo_ready, v * 2 + (n + 1 + NZ + unit0))
                for k in range(2):
                    pe.wait_ge(m_taken, v * 4 + (2 * n + k + 1 + 2 * unit0))
                    product(PV[k], n, KC * k, range(KC), rhs_hi, rhs_lo, hooks and hooks[k]).then_inc(tile_done, 1)

            with pe.Fori(0, NA // 4) as v:
                for n in range(2):
                    merge_unit(v, n, 0, o_hi, o_lo)

            def var():
                pe.wait_ge(csq_ready, 1)
                spread(TO, ones, ctmp).then_inc(var_ready, 1)

            for n in range(2):
                merge_unit(0, n, NA // 2, o_hi, o_lo, ({KC - 1: var}, None) if n == 0 else None)
            with pe.Fori(1, NA // 4) as v:
                for n in range(2):
                    merge_unit(v, n, NA // 2, o_hi, o_lo)
            pe.wait_ge(cn_ready, KC - 1)
            for n in range(2):
                merge_unit(0, n, NA, c_hi, c_lo, ({KC - 2: lambda: pe.wait_ge(cn_ready, KC)}, None) if n == 0 else None)
            with pe.Fori(1, NC_ // 2) as v:
                for n in range(2):
                    merge_unit(v, n, NA, c_hi, c_lo)

            def out_unit(v, n, hooks=None):
                pe.wait_ge(lo_ready, v * 2 + (n + 1 + U_OUT))
                pe.wait_ge(x2_ready, v * 2 + (n + 1))
                product(PV[n], n, 0, range(KD), m_hi, m_lo, hooks).then_inc(unit_done, 1)

            def last_merged():
                pe.wait_ge(merged_ready, KD)
                pe.wait_ge(m_taken, 2 + 2 * KD)

            pe.wait_ge(merged_ready, KD - 1)
            out_unit(0, 0, {KD - 2: last_merged})
            out_unit(0, 1)
            with pe.Fori(1, NO // 2) as v:
                for n in range(2):
                    out_unit(v, n)

            def rms2():
                pe.wait_ge(osum_ready, 1)
                spread(S, ones, osq).then_inc(ostat_ready, 1)

            pe.wait_ge(h2_ready, KD - 1)
            for n in range(2):
                pe.wait_ge(lo_ready, n + 1 + U_PQ)
                pe.wait_ge(x2_ready, n + 1 + NO)
                hooks = {7: rms2, KD - 2: lambda: pe.wait_ge(h2_ready, KD)} if n == 0 else None
                product(PV[n], n, 0, range(KD), h2_hi, h2_lo, hooks).then_inc(unit_done, 1)
            with pe.Fori(1, NQ // 2) as v:
                for n in range(2):
                    pe.wait_ge(lo_ready, v * 2 + (n + 1 + U_PQ))
                    pe.wait_ge(qp_ready, v * 2 + (n - 1))
                    product(PV[n], n, 0, range(KD), h2_hi, h2_lo).then_inc(unit_done, 1)
            pe.wait_ge(qp_ready, NQ)
            pe.wait_ge(late_loaded, 32)

            def u_unit(v, n, hooks=None):
                pe.wait_ge(lo_ready, v * 2 + (n + 1 + U_PU))
                pe.wait_ge(ab_full, v * 2 + (n + 1))
                product(PV[n], n, 0, range(KD), h2_hi, h2_lo, hooks).then_inc(unit_done, 1)

            for tt in range(TT):
                w = TS if tt == TT - 1 else P
                if tt:
                    pe.wait_ge(chosen_taken, tt)
                for s, bank in ((0, S), (1, TO)):
                    d = slice(s * DH, (s + 1) * DH)
                    for h in range(NH):
                        last = mm(bank[0:w, h // 4, (h % 4) * P:(h % 4 + 1) * P], qp[d, h, tt * P:tt * P + w], ksb[d, :],
                                  start=True, stop=True)
                last.then_inc(scores_ready, 1)
                with pe.Fori(0, TOPK_UNITS // 2 - 1) as v:
                    for n in range(2):
                        u_unit(v + tt * TOPK_UNITS // 2, n)

                def choices_t():
                    pe.wait_ge(chosen, tt + 1)
                    for x, src in enumerate((ssub[:, :], isel[:, 0, :], isel[:, 1, :])):
                        last = nc.tensor.transpose(S[:, 0, x * P:x * P + w], src[0:w, :], ident[0:w, 0:w])
                    last.then_inc(chosen_t, 1)

                def gate_sums():
                    pe.wait_ge(chosen_taken, TT)
                    spread(TO, late_sb[:, L_BLK16:L_BLK16 + P], e_t).then_inc(gsum_ready, 1)

                v_end = (tt + 1) * TOPK_UNITS // 2 - 1
                u_unit(v_end, 0, {3: choices_t})
                u_unit(v_end, 1, {1: gate_sums} if tt == TT - 1 else None)

            v0 = TT * TOPK_UNITS // 2
            with pe.Fori(0, NGB // 2) as v:
                for b in range(2):
                    for n in range(2):
                        def gates(x, b=b, n=n):
                            gq, t = 4 * b + 2 * n + x // 4, x % 4
                            if t == 0:
                                pe.wait_ge(oh_ready, v * 8 + (gq + 1))
                                pe.wait_ge(grp_taken, v * 8 + (gq + 1))
                            sl = 4 * (gq % 2) + t
                            out = (S, TO)[gq % 2][:, t // 2, (t % 2) * 2 * P:(t % 2 + 1) * 2 * P]
                            last = mm(out, oh2[:, sl, :], oh1[:, sl, :, :].rearrange("p h c -> p (h c)"), start=True, stop=True)
                            if t == 3:
                                last.then_inc(grp_done, 1)
                        u_unit(v * 2 + (v0 + b), n, {2 * x + 1: (lambda x=x, g=gates: g(x)) for x in range(8)})
            v1 = v0 + NGB
            with pe.Fori(0, NU // 2 - v1) as v:
                for n in range(2):
                    u_unit(v + v1, n)

            pe.wait_ge(ab_full, 2 + NU)
            with pe.Fori(0, NGRP // 2) as v:
                for b in range(2):
                    pe.wait_ge(w_prepped, v * (2 * GRP) + (b + 1) * GRP)
                    for n in range(GRP):
                        pe.wait_ge(lo_ready, v * (2 * GRP) + (b * GRP + n + 1 + U_PV))
                        for k in range(2):
                            pe.wait_ge(acc_added, v * (2 * KD) + (b * KD + 2 * n + k + 1))
                            last = None
                            for c in range(GRP):
                                o = (c * 2 + k) * P
                                wh, wl = w_hi[:, n % 2, o:o + P], w_lo[:, n % 2, o:o + P]
                                for y, (a, r_) in enumerate(((wh, wt_hi), (wh, wt_lo), (wl, wt_hi))):
                                    for f in range(2):
                                        last = mm(PV[k][:, f, :], a, r_[b][:, c, f * HT:(f + 1) * HT],
                                                  start=(c == 0 and y == 0), stop=(c == GRP - 1 and y == 2))
                            last.then_inc(tile_done, 1)


def _constants():
    half = DH // 2
    inv = (10000.0 ** (-np.arange(half, dtype=np.float32) / half)).astype(np.float32)
    ang = np.arange(TP, dtype=np.float32)[None, :] * np.tile(inv, P // half)[:, None]
    i = np.arange(P)
    blk = (i[:, None] // DH == i[None, :] // DH).astype(np.float32)
    perm = np.zeros((P, P), np.float32)
    for m in range(P):
        if m % DH < half:
            perm[m + half, m] = -1.0
        else:
            perm[m - half, m] = 1.0
    c = np.zeros((P, C_END), np.float32)
    c[:, C_COS:C_COS + TP] = np.cos(ang)
    c[:, C_SIN:C_SIN + TP] = np.sin(ang)
    c[:, C_ID:C_ID + P] = np.eye(P)
    c[:, C_BLK:C_BLK + P] = blk
    c[:, C_PERM:C_PERM + P] = perm
    c[:, C_ONES:C_ONES + P] = 1.0
    c[:, C_NEG:C_NEG + 64] = -1e30
    late = np.zeros((P, L_END), np.float32)
    late[:, L_IOTA:L_IOTA + P] = i[None, :]
    late[:, L_IOTA16:L_IOTA16 + 16] = np.arange(16)[None, :]
    late[:, L_BLK16:L_BLK16 + P] = i[:, None] // TOPK == i[None, :] // TOPK
    return c, late


def _tiles(w):
    k, n = w.shape
    return w.reshape(k // P, P, n // P, P).transpose(2, 1, 0, 3)


def kernel(**inputs):
    import concourse.bacc as _bacc
    from concourse.bass_utils import run_bass_kernel_spmd as _run

    a = {k: np.asarray(v) for k, v in inputs.items()}
    f = np.float32
    z = _tiles(a["w_in"][0])
    order = []
    for h in range(NH):
        order += [16 + h, 24 + h, 32 + h, h, 8 + h, 40 + 2 * h, 41 + 2 * h, 56 + 2 * h, 57 + 2 * h]
    w_all = np.empty((UNITS, P, UNITW), a["w_in"].dtype)
    w_all[:NZ] = z[order].reshape(NZ, P, UNITW)
    for u0, name in ((U_ATT, "w_attn_out"), (U_ATT + NA, "w_conv_out")):
        t = _tiles(a[name][0]).reshape(NA, 2, P, KC * P).transpose(0, 2, 1, 3)
        w_all[u0:u0 + NA] = t.reshape(NA, P, UNITW)
    w_all[U_OUT:U_PQ] = _tiles(a["w_out"][0]).reshape(NO, P, UNITW)
    w_all[U_PQ:U_PU] = _tiles(a["peer_wq"][0]).reshape(NQ, P, UNITW)
    w_all[U_PU:U_PV] = a["peer_u"][0].reshape(NU, P, KD, P).transpose(0, 3, 2, 1).reshape(NU, P, UNITW)
    w_all[U_PV:] = a["peer_v"][0].reshape(NGRP, GRP, P, 8, DM // 8).transpose(0, 3, 2, 1, 4).reshape(NV, P, UNITW)

    x = np.concatenate([a["x_prompt"][0], a["x_sample"][0]], axis=0)
    x_t = np.ascontiguousarray(x.T.reshape(KD, P, T).transpose(1, 0, 2))
    consts, late = _constants()
    params = np.concatenate([
        a["norm1_g"][0].reshape(KD, P).T, a["norm2_g"][0].reshape(KD, P).T,
        a["conv_dw_w"][0].reshape(TAPS, NH, P).transpose(2, 1, 0).reshape(P, NH * TAPS),
        a["conv_dw_b"][0].reshape(NH, P).T, a["conv_ln_g"][0].reshape(NH, P).T, a["conv_ln_b"][0].reshape(NH, P).T,
        np.tile(a["q_norm_g"][0], 2)[:, None], np.tile(a["k_norm_g"][0], 2)[:, None], a["subln_g"][0][:, None]], axis=1)
    lams = np.broadcast_to(np.stack([a["lambda_q1"][0], a["lambda_q2"][0], a["lambda_k1"][0], a["lambda_k2"][0]])[None],
                           (P, 4, DH))
    keys_t = np.concatenate([a["peer_k1"][0].T, a["peer_k2"][0].T], axis=0)
    past_k = a["cache_attn_k"][0, 0].transpose(1, 2, 3, 0).reshape(NH, P, PAST)
    past_v = a["cache_attn_v"][0, 0].reshape(PAST // P, P, NH, P).transpose(2, 1, 0, 3)
    hist = a["state_conv"][0, 0].T.reshape(NH, P, HIST)
    ins = dict(w_all=w_all, x_t=x_t, consts=consts, late=late, params=params, lams=lams, keys_t=keys_t,
               past_k=past_k, past_v=past_v, hist=hist)
    outs = dict(y_t=(KD, P, T), k_t=(NH, P, T), v_n=(T, NH, P), cst_p=(NH, P, HIST), cst_s=(NH, P, HIST))

    nc = _bacc.Bacc("TRN2", target_bir_lowering=False, num_devices=1)
    arrays = {k: np.ascontiguousarray(v) for k, v in ins.items()}
    aps = {k: nc.dram_tensor(k, v.shape, mybir.dt.from_np(v.dtype), kind="ExternalInput").ap() for k, v in arrays.items()}
    aps |= {k: nc.dram_tensor(k, s, F32, kind="ExternalOutput").ap() for k, s in outs.items()}
    build(nc, **aps)
    r = _run(nc, [arrays], core_ids=[0]).results[0]

    y = r["y_t"].reshape(DM, T).T
    k = r["k_t"].reshape(NH, 2, DH, T).transpose(3, 0, 1, 2)
    v = r["v_n"]

    def state(s):
        return s.reshape(NH * P, HIST).T[None, None]

    return (y[:TP][None], y[TP:][None], k[:TP][None, None], v[:TP][None, None], state(r["cst_p"]),
            k[TP:][None, None], v[TP:][None, None], state(r["cst_s"]))
```
